# Optimizing a Trainium2 kernel written in Bass

```python
import math
import jax, jax.numpy as jnp
from jax import lax
import numpy as np

D_MODEL = 1024
BATCH = 1
SEQ = 512
DEPTH = 1

MEM_TOKENS = 256
D_FF = 2816
NORM_EPS = 1e-6

GDN_HEADS = 4
GDN_HEAD_DIM = 128
GDN_WIDTH = GDN_HEADS * GDN_HEAD_DIM
GDN_CONV = 4
GDN_CHUNK = 64

MOBA_HEADS = 4
MOBA_HEAD_DIM = 64
MOBA_WIDTH = MOBA_HEADS * MOBA_HEAD_DIM
MOBA_BLOCK = 256
MOBA_TOPK = 3
MOBA_Q_BLOCK = 128

MEM_HEADS = 4
MEM_HEAD_DIM = 64
MEM_WIDTH = MEM_HEADS * MEM_HEAD_DIM

D_MIX = GDN_WIDTH + MOBA_WIDTH + MEM_WIDTH
IN_SPLITS = (GDN_WIDTH, GDN_WIDTH, GDN_WIDTH, GDN_WIDTH, GDN_HEADS, GDN_HEADS,
             MOBA_WIDTH, MOBA_WIDTH, MOBA_WIDTH, MEM_WIDTH)

kernel_name = "hymba_gdn_moba_macaron_layer"

def rms_norm(x, gain, eps=NORM_EPS):
    xf = x.astype(jnp.float32)
    y = xf * lax.rsqrt(jnp.mean(xf * xf, axis=-1, keepdims=True) + eps)
    return (y * gain.astype(jnp.float32)).astype(x.dtype)

def l2_normalize(x, eps=NORM_EPS):
    return x * lax.rsqrt(jnp.sum(x * x, axis=-1, keepdims=True) + eps)

def swiglu_ffn(x, gain, w_gate, w_up, w_down):
    h = rms_norm(x, gain)
    return (jax.nn.silu(h @ w_gate) * (h @ w_up)) @ w_down

def causal_depthwise_conv(x, w):
    k_len, ch = w.shape
    return lax.conv_general_dilated(x, w[:, None, :], window_strides=(1,), padding=[(k_len - 1, 0)],
                                    dimension_numbers=("NWC", "WIO", "NWC"), feature_group_count=ch)

def alibi_slopes(n_heads):
    return 2.0 ** (-8.0 * jnp.arange(1, n_heads + 1, dtype=jnp.float32) / n_heads)

def gated_deltanet(q, k, v, z, a, b, conv_w, a_log, dt_bias, out_gain):
    f32 = jnp.float32
    bsz, seq, _ = q.shape
    H, Dh, C = GDN_HEADS, GDN_HEAD_DIM, GDN_CHUNK
    n_chunks = seq // C
    qkv = jax.nn.silu(causal_depthwise_conv(jnp.concatenate([q, k, v], axis=-1), conv_w))
    qkv = qkv.astype(f32).reshape(bsz, seq, 3, H, Dh)
    q = l2_normalize(qkv[:, :, 0]) * Dh ** -0.5
    k = l2_normalize(qkv[:, :, 1])
    v = qkv[:, :, 2]
    beta = jax.nn.sigmoid(b.astype(f32))
    g = -jnp.exp(a_log.astype(f32)) * jax.nn.softplus(a.astype(f32) + dt_bias.astype(f32))

    def chunks(t):
        t = t.reshape((bsz, n_chunks, C) + t.shape[2:])
        return jnp.moveaxis(jnp.moveaxis(t, 1, 0), 3, 2)

    qc, kc, vc = chunks(q), chunks(k), chunks(v)
    bc = chunks(beta)
    gc = jnp.cumsum(chunks(g), axis=-1)
    lower = jnp.tril(jnp.ones((C, C), dtype=bool))
    strict = jnp.tril(jnp.ones((C, C), dtype=bool), -1)
    diff = gc[..., :, None] - gc[..., None, :]
    decay = jnp.where(lower, jnp.exp(jnp.where(lower, diff, 0.0)), 0.0)
    k_beta = kc * bc[..., None]
    a_mat = jnp.where(strict, jnp.einsum("nbhid,nbhjd->nbhij", k_beta, kc) * decay, 0.0)
    l_mat = a_mat + jnp.eye(C, dtype=f32)
    u = lax.linalg.triangular_solve(l_mat, vc * bc[..., None], left_side=True, lower=True,
                                    unit_diagonal=True)
    w = lax.linalg.triangular_solve(l_mat, k_beta * jnp.exp(gc)[..., None], left_side=True,
                                    lower=True, unit_diagonal=True)
    qk_intra = jnp.einsum("nbhid,nbhjd->nbhij", qc, kc) * decay

    def step(state, inp):
        q_i, k_i, u_i, w_i, g_i, a_i = inp
        v_new = u_i - jnp.einsum("bhcd,bhde->bhce", w_i, state)
        o_i = (jnp.einsum("bhcd,bhde->bhce", q_i * jnp.exp(g_i)[..., None], state)
               + jnp.einsum("bhij,bhje->bhie", a_i, v_new))
        g_last = g_i[..., -1]
        state = (state * jnp.exp(g_last)[..., None, None]
                 + jnp.einsum("bhcd,bhce->bhde", k_i * jnp.exp(g_last[..., None] - g_i)[..., None], v_new))
        return state, o_i

    state0 = jnp.zeros((bsz, H, Dh, Dh), f32)
    _, o = lax.scan(step, state0, (qc, kc, u, w, gc, qk_intra))
    o = jnp.moveaxis(jnp.moveaxis(o, 0, 1), 2, 3).reshape(bsz, seq, H, Dh)
    o = rms_norm(o, out_gain) * jax.nn.silu(z.astype(f32).reshape(bsz, seq, H, Dh))
    return o.reshape(bsz, seq, H * Dh)

def moba_attention(q, k, v, q_gain, k_gain):
    f32 = jnp.float32
    bsz, seq, _ = q.shape
    H, Dh, BLK, QB = MOBA_HEADS, MOBA_HEAD_DIM, MOBA_BLOCK, MOBA_Q_BLOCK
    t_pad = -(-seq // BLK) * BLK
    n_blocks = t_pad // BLK
    n_qblocks = t_pad // QB
    topk = min(MOBA_TOPK, n_blocks)
    bh = bsz * H

    def heads(t, gain=None):
        t = t.reshape(bsz, seq, H, Dh)
        if gain is not None:
            t = rms_norm(t, gain)
        t = t.astype(f32).transpose(0, 2, 1, 3).reshape(bh, seq, Dh)
        return jnp.pad(t, ((0, 0), (0, t_pad - seq), (0, 0)))

    qh, kh, vh = heads(q, q_gain), heads(k, k_gain), heads(v)
    kb = kh.reshape(bh, n_blocks, BLK, Dh)
    vb = vh.reshape(bh, n_blocks, BLK, Dh)
    k_mean = jnp.mean(kb, axis=2)
    slopes = jnp.broadcast_to(alibi_slopes(H), (bsz, H)).reshape(bh)
    scale = Dh ** -0.5
    key_offs = jnp.arange(BLK)
    q_blocks = qh.reshape(bh, n_qblocks, QB, Dh).transpose(1, 0, 2, 3)

    def one_query_block(args):
        q_blk, c = args
        t_pos = c * QB + jnp.arange(QB)
        own = (c * QB) // BLK
        gate = jnp.einsum("nqd,nbd->nqb", q_blk, k_mean)
        gate = jnp.where(jnp.arange(n_blocks) < own, gate, -jnp.inf)
        _, idx = lax.top_k(gate, topk)
        valid = idx < own
        k_sel = jax.vmap(lambda blocks, ids: blocks[ids])(kb, idx)
        v_sel = jax.vmap(lambda blocks, ids: blocks[ids])(vb, idx)
        dist_sel = (t_pos[None, :, None, None] - (idx[..., None] * BLK + key_offs)).astype(f32)
        s_sel = (jnp.einsum("nqd,nqrkd->nqrk", q_blk, k_sel) * scale
                 - slopes[:, None, None, None] * dist_sel)
        s_sel = jnp.where(valid[..., None], s_sel, -jnp.inf).reshape(bh, QB, topk * BLK)
        k_own = lax.dynamic_index_in_dim(kb, own, axis=1, keepdims=False)
        v_own = lax.dynamic_index_in_dim(vb, own, axis=1, keepdims=False)
        dist_own = (t_pos[:, None] - (own * BLK + key_offs)[None, :]).astype(f32)
        s_own = jnp.einsum("nqd,nkd->nqk", q_blk, k_own) * scale - slopes[:, None, None] * dist_own
        s_own = jnp.where(dist_own >= 0, s_own, -jnp.inf)
        p = jax.nn.softmax(jnp.concatenate([s_sel, s_own], axis=-1), axis=-1)
        p_sel = p[..., :topk * BLK].reshape(bh, QB, topk, BLK)
        p_own = p[..., topk * BLK:]
        return (jnp.einsum("nqrk,nqrkd->nqd", p_sel, v_sel)
                + jnp.einsum("nqk,nkd->nqd", p_own, v_own))

    out = lax.map(one_query_block, (q_blocks, jnp.arange(n_qblocks)))
    out = out.transpose(1, 0, 2, 3).reshape(bsz, H, t_pad, Dh)[:, :, :seq]
    return out.transpose(0, 2, 1, 3).reshape(bsz, seq, H * Dh)

def memory_attention(q, mem_h, w_kv, q_gain, k_gain):
    f32 = jnp.float32
    bsz, seq, _ = q.shape
    n_mem = mem_h.shape[1]
    H, Dh = MEM_HEADS, MEM_HEAD_DIM
    k, v = jnp.split(mem_h @ w_kv, 2, axis=-1)
    qh = rms_norm(q.reshape(bsz, seq, H, Dh), q_gain).astype(f32)
    kh = rms_norm(k.reshape(bsz, n_mem, H, Dh), k_gain).astype(f32)
    vh = v.reshape(bsz, n_mem, H, Dh).astype(f32)
    p = jax.nn.softmax(jnp.einsum("bthd,bmhd->bhtm", qh, kh) * Dh ** -0.5, axis=-1)
    return jnp.einsum("bhtm,bmhd->bthd", p, vh).reshape(bsz, seq, H * Dh)

def setup_inputs(seed: int = 0) -> dict:
    key = jax.random.key(seed)
    ks = jax.random.split(key, 24)
    f32 = jnp.float32
    L = DEPTH
    d_in = sum(IN_SPLITS)

    def dense(k, fan_in, fan_out):
        return jax.random.normal(k, (L, fan_in, fan_out), f32) * fan_in ** -0.5

    def gain(k, n):
        return 1.0 + 0.02 * jax.random.normal(k, (L, n), f32)

    dt = jnp.exp(jax.random.uniform(ks[8], (L, GDN_HEADS), f32, math.log(1e-3), math.log(1e-1)))
    return {
        "x": jax.random.normal(ks[0], (BATCH, SEQ, D_MODEL), f32),
        "mem": jax.random.normal(ks[1], (BATCH, MEM_TOKENS, D_MODEL), f32),
        "ffn1_norm": gain(ks[2], D_MODEL),
        "ffn1_w_gate": dense(ks[3], D_MODEL, D_FF),
        "ffn1_w_up": dense(ks[4], D_MODEL, D_FF),
        "ffn1_w_down": dense(ks[5], D_FF, D_MODEL),
        "mix_norm": gain(ks[6], D_MODEL),
        "w_in": dense(ks[7], D_MODEL, d_in),
        "gdn_conv_w": jax.random.normal(ks[9], (L, GDN_CONV, 3 * GDN_WIDTH), f32) * GDN_CONV ** -0.5,
        "gdn_a_log": jnp.log(jax.random.uniform(ks[10], (L, GDN_HEADS), f32, 1.0, 16.0)),
        "gdn_dt_bias": dt + jnp.log(-jnp.expm1(-dt)),
        "gdn_out_norm": gain(ks[11], GDN_HEAD_DIM),
        "moba_q_norm": gain(ks[12], MOBA_HEAD_DIM),
        "moba_k_norm": gain(ks[13], MOBA_HEAD_DIM),
        "mem_norm": gain(ks[14], D_MODEL),
        "w_mem_kv": dense(ks[15], D_MODEL, 2 * MEM_WIDTH),
        "mem_q_norm": gain(ks[16], MEM_HEAD_DIM),
        "mem_k_norm": gain(ks[17], MEM_HEAD_DIM),
        "w_out": dense(ks[18], D_MIX, D_MODEL),
        "ffn2_norm": gain(ks[19], D_MODEL),
        "ffn2_w_gate": dense(ks[20], D_MODEL, D_FF),
        "ffn2_w_up": dense(ks[21], D_MODEL, D_FF),
        "ffn2_w_down": dense(ks[22], D_FF, D_MODEL),
    }

def reference(x, mem, ffn1_norm, ffn1_w_gate, ffn1_w_up, ffn1_w_down, mix_norm, w_in,
              gdn_conv_w, gdn_a_log, gdn_dt_bias, gdn_out_norm, moba_q_norm, moba_k_norm,
              mem_norm, w_mem_kv, mem_q_norm, mem_k_norm, w_out,
              ffn2_norm, ffn2_w_gate, ffn2_w_up, ffn2_w_down):
    split_at = np.cumsum(IN_SPLITS)[:-1].tolist()
    for l in range(DEPTH):
        x = x + 0.5 * swiglu_ffn(x, ffn1_norm[l], ffn1_w_gate[l], ffn1_w_up[l], ffn1_w_down[l])
        h = rms_norm(x, mix_norm[l])
        gq, gk, gv, gz, ga, gb, mq, mk, mv, cq = jnp.split(h @ w_in[l], split_at, axis=-1)
        y_gdn = gated_deltanet(gq, gk, gv, gz, ga, gb, gdn_conv_w[l], gdn_a_log[l], gdn_dt_bias[l],
                               gdn_out_norm[l])
        y_moba = moba_attention(mq, mk, mv, moba_q_norm[l], moba_k_norm[l])
        y_mem = memory_attention(cq, rms_norm(mem, mem_norm[l]), w_mem_kv[l], mem_q_norm[l], mem_k_norm[l])
        y = jnp.concatenate([y_gdn, y_moba, y_mem], axis=-1).astype(x.dtype)
        x = x + y @ w_out[l]
        x = x + 0.5 * swiglu_ffn(x, ffn2_norm[l], ffn2_w_gate[l], ffn2_w_up[l], ffn2_w_down[l])
    return x


_drawn_inputs = setup_inputs


def setup_inputs(seed=0):
    import zlib

    import numpy as np

    out = dict(_drawn_inputs(seed))
    spreads = {}
    factors = {'ffn1_norm': 5.773,
     'mix_norm': 4.022,
     'gdn_out_norm': 20.352,
     'moba_q_norm': 196.241,
     'moba_k_norm': 144.86,
     'mem_norm': 32.981,
     'mem_q_norm': 27.458,
     'mem_k_norm': 33.616,
     'ffn2_norm': 34.517}
    for name, (base, spread) in spreads.items():
        noise = np.random.default_rng([zlib.crc32(name.encode()), seed]).standard_normal(out[name].shape)
        drawn = base * np.exp(spread * noise) if base else spread * noise
        out[name] = __import__('jax').numpy.asarray(drawn.astype(out[name].dtype))
    for name, factor in factors.items():
        out[name] = (out[name] * factor).astype(out[name].dtype)
    return out
```

```python
from contextlib import ExitStack

import concourse.bass as bass
from concourse import mybir

F32 = mybir.dt.float32
F32R = mybir.dt.float32r
ALU = mybir.AluOpType
ACT = mybir.ActivationFunctionType
AX = mybir.AxisListType

P = 128
T = 512
NC_ = T // P
D = 1024
KD = D // P
M = 256
MC = M // P
FG = 2816 // 256
H = 4
DH = 64
EPS = 1e-6
SCALE = DH ** -0.5
LEVELS = 7
SLOPES = [2.0 ** (-8.0 * (h + 1) / H) for h in range(H)]

U_MEM = 0
U_FFN = [2, 2 + 3 * FG + 12 + 4]
U_IN = 2 + 3 * FG
U_OUT = U_IN + 12
UNITS = U_FFN[1] + 3 * FG
RAW = 2
RING = 3

C_ID, C_UP, C_ONE, C_NEG, C_LEV = 0, P, 2 * P, 3 * P, 4 * P
C_REL = C_LEV + LEVELS * P
C_SEL = C_REL + T
C_N = C_SEL + 2
S_G1, S_GM, S_G2, S_GMEM = 0, KD, 2 * KD, 3 * KD
S_CONV = 4 * KD
S_OG = S_CONV + 12 * 4
S_MQ, S_MK, S_CQ, S_CK = S_OG + 1, S_OG + 2, S_OG + 3, S_OG + 4
S_ALOG = S_OG + 5
S_DT = S_ALOG + H
S_N = S_DT + H


def build(nc, stream, x_in, mem_in, ab_in, small_in, const_in, out):
    with ExitStack() as ctx:
        arena_bytes = 208 * 1024
        arena = ctx.enter_context(nc.sbuf_tensor("arena", [P, (arena_bytes - 600) // 4], F32))
        base = (nc.sbuf_base - arena_bytes + 600 + 31) // 32 * 32
        cursor = [base]

        def place(name, shape, dt=F32, at=None):
            size = 4
            for n in shape[1:]:
                size *= n
            if at is None:
                at = cursor[0]
                cursor[0] += (size + 31) // 32 * 32
            return nc.alloc_sbuf_tensor_at(name, shape, dt, offset=at), at, at + (size + 31) // 32 * 32

        def sem(name):
            return ctx.enter_context(nc.semaphore(name))

        x, _, _ = place("x", [P, KD, T])
        ahi, a_hi0, _ = place("ahi", [P, KD, T], F32R)
        alo, a_lo0, _ = place("alo", [P, KD, T], F32R)
        raw, _, _ = place("raw", [P, RAW, 2048])
        whi, _, _ = place("whi", [P, RING, 2048], F32R)
        wlo, _, _ = place("wlo", [P, RING, 2048], F32R)
        rbc, _, _ = place("rbc", [P, T])
        cst, _, _ = place("cst", [P, C_N])
        small, _, _ = place("small", [P, S_N])
        abr, _, _ = place("abr", [P, KD, 8])
        abhi, _, _ = place("abhi", [P, KD, 8], F32R)
        ablo, _, _ = place("ablo", [P, KD, 8], F32R)
        rtm, _, _ = place("rtm", [P, 3, NC_])
        rmem, _, _ = place("rmem", [P, MC])
        msq_, _, _ = place("stat_mean", [P, 48])
        root, _, _ = place("stat_root", [P, 48])
        newt, _, _ = place("stat_newton", [P, 48])
        inv0, _, _ = place("stat_inv", [P, 48])
        rqk, _, _ = place("rqk", [P, 8, NC_])
        ratt, _, _ = place("ratt", [P, 6, NC_, 2])
        rmk, _, _ = place("rmk", [P, 2, MC, 2])
        gain_qk, _, _ = place("gain_qk", [P, 2])
        gates, _, _ = place("gates", [P, 16, 16])
        rowmax, _, _ = place("rowmax", [P, 4])
        negmax, _, _ = place("negmax", [P, 4])
        rowsum, _, _ = place("rowsum", [P, 4])
        rowinv, _, _ = place("rowinv", [P, 4])
        mid = cursor[0]

        qkv, _, _ = place("qkv", [P, 12, T])
        z, z_at, _ = place("z", [P, H, T])
        mq, mq_at, _ = place("mq", [P, 2, T])
        mk, _, _ = place("mk", [P, 2, T])
        cq, _, _ = place("cq", [P, 2, T])
        mv, _, _ = place("mv", [P, NC_, M])
        ck, _, _ = place("ck", [P, 2, M])
        cv, _, _ = place("cv", [P, MC, M])
        kt, kt_at, _ = place("kt", [P, NC_, H, P])
        pt, pt_at, _ = place("pt", [P, NC_, H, P])
        xt, xt_at, _ = place("xt", [P, NC_, H, P])
        dec, dec_at, _ = place("dec", [P, H, P])
        at_, _, _ = place("at", [P, 2, H, P])
        top = cursor[0]
        assert top <= base + arena_bytes - 600, (top, base + arena_bytes)
        cin, _, nxt = place("cin", [P, 2, T + 4], at=kt_at)
        cout, _, _ = place("cout", [P, 2, T], at=nxt)
        sqk, _, _ = place("sqk", [P, 4, T], at=xt_at)
        sqa, _, _ = place("sqa", [P, 6, T], at=kt_at)
        half = 4 * T * 4
        bm, _, nxt = place("bm", [P, 2, H, P], at=a_hi0 + half)
        ysb, _, _ = place("ysb", [P, 2, H, P], at=nxt)
        xn, _, nxt = place("xn", [P, 2, H, P], at=a_lo0 + half)
        egb, _, _ = place("egb", [P, H, P], at=nxt)
        sc, _, nxt = place("sc", [P, 2, T], at=a_hi0)
        ptr, _, _ = place("ptr", [P, 2, NC_, P], at=nxt)
        rsb, _, nxt = place("rsb", [P, H, P], at=a_lo0)
        vsb, _, nxt = place("vsb", [P, H, P], at=nxt)
        state, _, _ = place("state", [P, 2, H, P], at=nxt)
        prob, _, _ = place("prob", [P, 3, T], at=dec_at)
        gbuf, _, nxt = place("gbuf", [P, 2, T], at=mid)
        hhi, _, nxt = place("hhi", [P, 4, T], F32R, at=nxt)
        hlo, _, nxt = place("hlo", [P, 4, T], F32R, at=nxt)
        sqx, _, sqx_end = place("sqx", [P, KD, T], at=z_at)
        memx, _, nxt = place("memx", [P, KD, M], at=nxt)
        assert nxt <= z_at + 1024 * 32
        memx, _, nxt = place("memx2", [P, KD, M], at=kt_at)
        memhi, _, nxt = place("memhi", [P, KD, M], F32R, at=nxt)
        memlo, _, nxt = place("memlo", [P, KD, M], F32R, at=nxt)
        memsq, _, nxt2 = place("memsq", [P, KD, M], at=mid)
        mksq, _, _ = place("mksq", [P, 2, M], at=nxt2)
        abt, _, _ = place("abt", [8, T], at=dec_at)
        assert nxt <= top

        psum = [ctx.enter_context(nc.psum_tensor(f"bank{i}", [P, T], F32)) for i in range(8)]

        ident, upper = cst[:, C_ID:C_ID + P], cst[:, C_UP:C_UP + P]
        ones, negmask = cst[:, C_ONE:C_ONE + P], cst[:, C_NEG:C_NEG + P]
        headsel = cst[:, C_SEL:C_SEL + 2]

        def level(l):
            return cst[:, C_LEV + l * P:C_LEV + (l + 1) * P]

        def over_heads(ap):
            return ap.unsqueeze(1).broadcast_to([P, H, P])

        def heads(bank):
            return psum[bank][:, :].rearrange("p (h t) -> p h t", h=H)

        def col(c):
            return small[:, c:c + 1]

        (G_A, G_B, G_NEG, G_EXP, G_LN, G_G, G_EB, G_BETA, G_GC, G_GL, G_GT, G_EG, G_EGL, G_ET,
         G_RKB, G_SR) = range(16)

        def gate(n, m=1):
            return gates[:, n:n + m, :]

        def gate_hc(n):
            return gates[:, n, :].rearrange("p (h c) -> p h c", h=H)

        def gcol(n, h, c):
            return gates[:, n, h * NC_ + c:h * NC_ + c + 1]

        cst_in, small_sem, mem_sem, ab_sem, out_done = (
            sem(n) for n in ("cst_in", "small_sem", "mem_sem", "ab_sem", "out_done"))
        x_sem = [sem(f"x_in{i}") for i in range(4)]
        raw_in = [sem(f"raw_in{i}") for i in range(RAW)]
        w_hi, w_lo, w_used = sem("w_hi"), sem("w_lo"), sem("w_used")
        dve_chain, act_chain = sem("dve_chain"), sem("act_chain")
        ab_hi, ab_lo = sem("ab_hi"), sem("ab_lo")
        mem_hi, mem_lo, mem_sq, mem_stat = sem("mem_hi"), sem("mem_lo"), sem("mem_sq"), sem("mem_stat")
        ck_ps, cv_ps, rm_ready, rmbc_ps, rmbc_sb = (
            sem(n) for n in ("ck_ps", "cv_ps", "rm_ready", "rmbc_ps", "rmbc_sb"))
        ck_raw, ck_sq, ck_stat, rmk_ready, ckbc_ps, ck_ready = (
            sem(n) for n in ("ck_raw", "ck_sq", "ck_stat", "rmk_ready", "ckbc_ps", "ck_ready"))
        mean_ready, root_ready = sem("mean_ready"), sem("root_ready")
        a_hi, a_lo, sq_ready, stat_done = sem("a_hi"), sem("a_lo"), sem("sq_ready"), sem("stat_done")
        rtm_ready, rbc_ps, r_ready = sem("rtm_ready"), sem("rbc_ps"), sem("r_ready")
        gate_done, gate_scaled, silu_done, up_done = (
            sem(n) for n in ("gate_done", "gate_scaled", "silu_done", "up_done"))
        silu_scaled, h_done, h_hi, h_lo = sem("silu_scaled"), sem("h_done"), sem("h_hi"), sem("h_lo")
        down_done, x_added = sem("down_done"), sem("x_added")
        p_done, p_evac, conv_done, qkv_ready = sem("p_done"), sem("p_evac"), sem("conv_done"), sem("qkv_ready")
        sqk_ready, sqk_used, z_ready = sem("sqk_ready"), sem("sqk_used"), sem("z_ready")
        sqa_ready, sqa_used = sem("sqa_ready"), sem("sqa_used")
        ab_ps, ab_sb, ab_tm, ab_read = sem("ab_ps"), sem("ab_sb"), sem("ab_tm"), sem("ab_read")
        g_dve, g_act, g_pe = sem("g_dve"), sem("g_act"), sem("g_pe")
        gates_ready, rqk_ready, ratt_ready = sem("gates_ready"), sem("rqk_ready"), sem("ratt_ready")
        prep_ps = [sem(f"prep_ps{i}") for i in range(6)]
        dpre, dexp, egb_ready, egb_used = sem("dpre"), sem("dexp"), sem("egb_ready"), sem("egb_used")
        g_read, rb_read, kk_read, qk_read = sem("g_read"), sem("rb_read"), sem("kk_read"), sem("qk_read")
        kt_ready, bv_ready, qe_ready, at_ready, pt_ready = (
            sem(n) for n in ("kt_ready", "bv_ready", "qe_ready", "at_ready", "pt_ready"))
        mkbc_ps, mk_ready = sem("mkbc_ps"), sem("mk_ready")
        b_ready, y_ps, y_sb, xp_ps, xtp_ps, x_upd, xt_upd = (
            sem(n) for n in ("b_ready", "y_ps", "y_sb", "xp_ps", "xtp_ps", "x_upd", "xt_upd"))
        s_ps, nm_ready, exp_done, p_norm, pt_ps, pt_sb, pv_done, yb_hi, yb_lo = (
            sem(n) for n in ("s_ps", "nm_ready", "exp_done", "p_norm", "pt_ps", "pt_sb", "pv_done",
                             "yb_hi", "yb_lo"))
        ks_ps, r_sb, v_ps, v_sb, o_ps, o_sb, kv_ps, s_upd = (
            sem(n) for n in ("ks_ps", "r_sb", "v_ps", "v_sb", "o_ps", "o_sb", "kv_ps", "s_upd"))
        o_stat, ro_ready, obc_ps, y_tm, y_hi, y_lo = (
            sem(n) for n in ("o_stat", "ro_ready", "obc_ps", "y_tm", "y_hi", "y_lo"))
        wo_ps, xo_added = sem("wo_ps"), sem("xo_added")

        def wslice(parts, u, k, c0, n, width):
            s = u % RING
            return parts[:, s, k * width + c0:k * width + c0 + n]

        jobs = [(kind, h, c) for c in range(NC_) for kind in ("moba", "mem") for h in range(H)]
        NJ = len(jobs)
        JC = 2 * H

        block = ctx.enter_context(nc.Block())

        @block.sync
        def _(sp):
            sp.dma_start(small[:], small_in).then_inc(small_sem, 16)
            sp.dma_start(memx[:], mem_in).then_inc(mem_sem, 16)
            sp.dma_start(raw[:, 0, :], stream[0:1, :, :].rearrange("o p n -> (o p) n")).then_inc(raw_in[0], 16)
            sp.dma_start(cst[:], const_in).then_inc(cst_in, 16)
            for i in range(4):
                sp.dma_start(x[:, 2 * i:2 * i + 2, :], x_in[:, 2 * i:2 * i + 2, :]).then_inc(x_sem[i], 16)
                if i == 0:
                    sp.dma_start(raw[:, 1, :], stream[1:2, :, :].rearrange("o p n -> (o p) n")
                                 ).then_inc(raw_in[1], 16)
            sp.dma_start(abr[:], ab_in).then_inc(ab_sem, 16)
            with sp.Fori(1, UNITS // RAW) as i:
                for s in range(RAW):
                    sp.wait_ge(w_lo, RAW * i + (s + 1 - RAW))
                    sp.dma_start(raw[:, s, :], stream[bass.ds(i * RAW + s, 1), :, :].rearrange("o p n -> (o p) n")
                                 ).then_inc(raw_in[s], 16)
            for d in range(KD):
                sp.wait_ge(x_added, 2 * KD * FG - KD + d + 1)
                sp.dma_start(out[:, d, :], x[:, d, :]).then_inc(out_done, 16)
            sp.wait_ge(out_done, 16 * KD)

        @block.gpsimd
        def _(pool):
            period = RAW * RING

            def split(u, count):
                pool.wait_ge(w_hi, count + 1)
                nc.gpsimd.tensor_tensor(wlo[:, u % RING, :], raw[:, u % RAW, :],
                                        whi[:, u % RING, :].bitcast(F32), ALU.subtract).then_inc(w_lo, 1)

            with pool.Fori(0, UNITS // period) as i:
                for s in range(period):
                    split(s, i * period + s)

        @block.scalar
        def _(act):
            A = nc.scalar

            def weight_hi(u, count=None, loads=None):
                count = u if count is None else count
                loads = u // RAW if loads is None else loads
                act.wait_ge(raw_in[u % RAW], loads * 16 + 16)
                if not (isinstance(count, int) and count < RING):
                    act.wait_ge(w_used, count + (1 - RING))
                A.activation(whi[:, u % RING, :], raw[:, u % RAW, :], ACT.Copy).then_inc(w_hi, 1)

            def sqrt(n, width):
                act.wait_ge(mean_ready, n + 1)
                A.activation(root[:, 0:width], msq_[:, 0:width], ACT.Sqrt).then_inc(root_ready, 1)

            def x_parts(stage, gain, ready):
                for d in range(KD):
                    ready(d)
                    A.activation(ahi[:, d, :], x[:, d, :], ACT.Copy, scale=col(gain + d)).then_inc(a_hi, 1)
                for d in range(KD):
                    A.activation(sqx[:, d, :], x[:, d, :], ACT.Square).then_inc(sq_ready, 1)

            act.wait_ge(small_sem, 16)
            act.wait_ge(mem_sem, 16)
            for k in range(KD):
                A.activation(memhi[:, k, :], memx[:, k, :], ACT.Copy, scale=col(S_GMEM + k)).then_inc(mem_hi, 1)
                if k == 1:
                    weight_hi(0)
            A.activation(memsq[:, :, :], memx[:, :, :], ACT.Square).then_inc(mem_sq, 1)
            weight_hi(1)
            weight_hi(2)
            sqrt(0, MC)
            act.wait_ge(rmbc_ps, 1)
            A.activation(rbc[:, 0:M], psum[2][:, 0:M], ACT.Copy).then_inc(rmbc_sb, 1)
            x_parts(0, S_G1, lambda d: act.wait_ge(x_sem[d // 2], 16))
            act.wait_ge(ck_raw, 2)
            act.wait_ge(mem_stat, 1)
            A.activation(mksq[:, :, :], ck[:, :, :], ACT.Square).then_inc(ck_sq, 1)
            weight_hi(3)
            act.wait_ge(ab_sem, 16)
            A.activation(abhi[:], abr[:], ACT.Copy).then_inc(ab_hi, 1)
            sqrt(1, 4 * MC)

            def ffn_step(f, i, b, with_weights=True):
                n0, u0 = 2 * FG * f, U_FFN[f]
                for a in range(2):
                    act.wait_ge(gate_scaled, 2 * i + (n0 + a + 1))
                    A.activation(gbuf[:, a, :], gbuf[:, a, :], ACT.Silu).then_inc(silu_done, 1)

                def hi(j):
                    weight_hi(u0 + 3 * i + j)

                hi(2)
                act.wait_ge(w_used, 3 * i + (u0 - 1))
                for a in range(2):
                    act.wait_ge(h_done, 2 * i + (n0 + a + 1))
                    A.activation(hhi[:, 2 * b + a, :], gbuf[:, a, :], ACT.Copy).then_inc(h_hi, 1)
                if with_weights:
                    hi(3)
                    hi(4)

            def ffn_pair(f, j):
                n0, u0 = 2 * FG * f, U_FFN[f]
                for b in range(2):
                    for a in range(2):
                        act.wait_ge(gate_scaled, 4 * j + (n0 + 2 * b + a + 1))
                        A.activation(gbuf[:, a, :], gbuf[:, a, :], ACT.Silu).then_inc(silu_done, 1)

                    def hi(m):
                        v = u0 + 3 * b + m
                        weight_hi(v, 6 * j + v, 3 * j + v // RAW)

                    hi(2)
                    act.wait_ge(w_used, 6 * j + (u0 + 3 * b - 1))
                    for a in range(2):
                        act.wait_ge(h_done, 4 * j + (n0 + 2 * b + a + 1))
                        A.activation(hhi[:, 2 * b + a, :], gbuf[:, a, :], ACT.Copy).then_inc(h_hi, 1)
                    hi(3)
                    hi(4)

            sqrt(2, NC_)
            with act.Fori(0, FG // 2) as j:
                ffn_pair(0, j)
            ffn_step(0, FG - 1, 0)

            x_parts(1, S_GM, lambda d: act.wait_ge(x_added, KD * (FG - 1) + d + 1))
            for n in range(12):
                weight_hi(U_IN + n + 2)
                if n == 0:
                    sqrt(3, NC_)
                for q in (2 * n, 2 * n + 1):
                    if q < 12:
                        act.wait_ge(conv_done, q + 1)
                        A.activation(qkv[:, q, :], cout[:, q % 2, :], ACT.Silu).then_inc(qkv_ready, 1)
                        if q < 8:
                            if q >= 4:
                                act.wait_ge(sqk_used, q - 3)
                            act.wait_ge(qkv_ready, q + 1)
                            A.activation(sqk[:, q % 4, :], qkv[:, q, :], ACT.Square).then_inc(sqk_ready, 1)
                    elif q < 16:
                        act.wait_ge(p_evac, q + 1)
                        A.activation(z[:, q - 12, :], z[:, q - 12, :], ACT.Silu).then_inc(z_ready, 1)
                    elif q < 22:
                        t = q - 16
                        src = (mq, mk, cq)[t // 2][:, t % 2, :]
                        act.wait_ge(p_evac, q + 1)
                        A.activation(sqa[:, t, :], src, ACT.Square).then_inc(sqa_ready, 1)
                if n == 7:
                    sqrt(4, 32)
                    act.wait_ge(g_dve, 1)
                    A.activation(gate(G_EXP), gate(G_NEG), ACT.Exp).then_inc(g_act, 1)
                    A.activation(gate(G_EB), gate(G_B), ACT.Exp, scale=-1.0).then_inc(g_act, 1)
                    A.activation(rowmax[:], small[:, S_ALOG:S_ALOG + H], ACT.Exp).then_inc(g_act, 1)
                    act.wait_ge(g_dve, 2)
                    A.activation(gate(G_LN), gate(G_EXP), ACT.Ln).then_inc(g_act, 1)
                    act.wait_ge(g_dve, 4)
                    A.activation(gate(G_EG, 3), gate(G_GC, 3), ACT.Exp).then_inc(g_act, 1)
            sqrt(5, 48)

            def prep(c):
                act.wait_ge(prep_ps[0], c + 1)
                if c >= 1:
                    act.wait_ge(egb_used, c)
                A.activation(egb[:], heads(0), ACT.Exp).then_inc(egb_ready, 1)
                act.wait_ge(dpre, c + 1)
                A.activation(dec[:], dec[:], ACT.Exp).then_inc(dexp, 1)
                act.wait_ge(prep_ps[4], c + 1)
                for h in range(H):
                    A.activation(kt[:, c, h, :], heads(0)[:, h, :], ACT.Copy,
                                 scale=gcol(G_ET, h, c)).then_inc(kt_ready, 1)

            def inverse(pair):
                for l in range(1, LEVELS):
                    for j in range(2):
                        n = pair * 2 * (LEVELS - 1) + (l - 1) * 2 + j
                        act.wait_ge(y_ps, n + 1)
                        A.activation(ysb[:, j, :, :], heads(4 + 2 * j), ACT.Copy).then_inc(y_sb, 1)

            act.wait_ge(gates_ready, 1)
            for pair in range(2):
                prep(2 * pair)
                prep(2 * pair + 1)
                inverse(pair)

            weight_hi(U_OUT + 2)
            for a in range(NJ + 3):
                if a < NJ:
                    kind, h, c = jobs[a]
                    act.wait_ge(nm_ready, a + 1)
                    if a >= 3:
                        act.wait_ge(pt_ps, a - 2)
                    if kind == "moba":
                        w = P * (c + 1)
                        A.activation(prob[:, a % 3, 0:w], sc[:, a % 2, 0:w], ACT.Exp, bias=negmax[:, a % 4:a % 4 + 1],
                                     scale=SLOPES[h], accum_out=rowsum[:, a % 4:a % 4 + 1]).then_inc(exp_done, 1)
                    else:
                        A.activation(prob[:, a % 3, 0:M], psum[4 + a % 2][:, 0:M], ACT.Exp,
                                     bias=negmax[:, a % 4:a % 4 + 1], scale=ratt[:, 4 + h // 2, c, h % 2:h % 2 + 1],
                                     accum_out=rowsum[:, a % 4:a % 4 + 1]).then_inc(exp_done, 1)
                if 2 <= a < NJ + 2:
                    kind, h, c = jobs[a - 2]
                    n = c + 1 if kind == "moba" else MC
                    act.wait_ge(pt_ps, a - 1)
                    if a >= 4:
                        act.wait_ge(pv_done, a - 3)
                    A.activation(ptr[:, a % 2, 0:n, :], heads(6)[:, 0:n, :], ACT.Copy).then_inc(pt_sb, 1)
                c, s = a // JC, a % JC
                if c < NC_ and s == 1:
                    act.wait_ge(v_ps, c + 1)
                    if c >= 1:
                        act.wait_ge(kv_ps, c)
                    A.activation(vsb[:], heads(1), ACT.Copy).then_inc(v_sb, 1)
                if c < NC_ and s == 3:
                    act.wait_ge(o_ps, c + 1)
                    A.activation(qkv[:, 0:H, c * P:(c + 1) * P], heads(2), ACT.Copy).then_inc(o_sb, 1)
                    A.activation(qkv[:, H:2 * H, c * P:(c + 1) * P], heads(2), ACT.Square).then_inc(o_sb, 1)
                if a >= JC + 2 and (a - 2) % JC == 0:
                    c = (a - 2) // JC - 1
                    act.wait_ge(pv_done, JC * (c + 1))
                    A.activation(ahi[:, 4:8, c * P:(c + 1) * P], heads(7), ACT.Copy).then_inc(yb_hi, 1)
            sqrt(6, 16)
            for h in range(H):
                act.wait_ge(y_tm, h + 1)
                if h == 0:
                    act.wait_ge(exp_done, NJ)
                A.activation(ahi[:, h, :], qkv[:, 8 + h, :], ACT.Copy).then_inc(y_hi, 1)
            for m in range(1, 4):
                weight_hi(U_OUT + m + 2)
            act.wait_ge(wo_ps, KD)
            x_parts(2, S_G2, lambda d: act.wait_ge(xo_added, d + 1))
            sqrt(7, NC_)
            with act.Fori(0, FG // 2) as j:
                ffn_pair(1, j)
            ffn_step(1, FG - 1, 0, with_weights=False)

        @block.vector
        def _(dve):
            V = nc.vector
            links = [0]

            def link(ins):
                links[0] += 1
                ins.then_inc(dve_chain, 1)
                dve.wait_ge(dve_chain, links[0])

            def mean(n, src, dst, scale):
                V.tensor_scalar(dst, src, scale, EPS, ALU.mult, ALU.add).then_inc(mean_ready, 1)
                dve.wait_ge(mean_ready, n + 1)

            def rsqrt(n, width, dst, done):
                m, y, t, i0 = msq_[:, 0:width], root[:, 0:width], newt[:, 0:width], inv0[:, 0:width]
                dve.wait_ge(root_ready, n + 1)
                link(V.reciprocal(i0, y))
                link(V.scalar_tensor_tensor(out=t, in0=m, scalar=-0.5, in1=i0, op0=ALU.mult, op1=ALU.mult))
                link(V.tensor_tensor(t, t, i0, ALU.mult))
                link(V.scalar_tensor_tensor(out=dst, in0=t, scalar=1.5, in1=i0, op0=ALU.add, op1=ALU.mult))
                V.tensor_copy(newt[:, 0:1], i0[:, 0:1]).then_inc(done, 1)

            def x_low(stage, gain, d):
                dve.wait_ge(a_hi, KD * stage + d + 1)
                V.scalar_tensor_tensor(out=alo[:, d, :], in0=x[:, d, :], scalar=col(gain + d),
                                       in1=ahi[:, d, :].bitcast(F32), op0=ALU.mult,
                                       op1=ALU.subtract).then_inc(a_lo, 1)

            def x_stat(stage, n):
                dve.wait_ge(stat_done, stage + 1)
                mean(n, psum[4][:, 0:NC_], msq_[:, 0:NC_], 1.0 / D)
                rsqrt(n, NC_, rtm[:, stage, :], rtm_ready)
                dve.wait_ge(rbc_ps, stage + 1)
                V.tensor_copy(rbc[:], psum[5][:]).then_inc(r_ready, 1)
                dve.wait_ge(r_ready, stage + 1)

            dve.wait_ge(small_sem, 16)
            V.tensor_tensor(gain_qk[:, 0:1], col(S_MQ), col(S_MK), ALU.mult).then_inc(dve_chain, 1)
            V.tensor_tensor(gain_qk[:, 1:2], col(S_CQ), col(S_CK), ALU.mult).then_inc(dve_chain, 1)
            links[0] += 2
            dve.wait_ge(dve_chain, links[0])
            for k in range(KD):
                dve.wait_ge(mem_hi, k + 1)
                V.scalar_tensor_tensor(out=memlo[:, k, :], in0=memx[:, k, :], scalar=col(S_GMEM + k),
                                       in1=memhi[:, k, :].bitcast(F32), op0=ALU.mult,
                                       op1=ALU.subtract).then_inc(mem_lo, 1)
            dve.wait_ge(mem_stat, 1)
            mean(0, psum[4][:, 0:MC], msq_[:, 0:MC], 1.0 / D)
            rsqrt(0, MC, rmem[:, :], rm_ready)
            dve.wait_ge(rm_ready, 1)
            dve.wait_ge(ck_ps, 2)
            dve.wait_ge(rmbc_sb, 1)
            for j in range(2):
                V.tensor_tensor(ck[:, j, :], psum[j][:, 0:M], rbc[:, 0:M], ALU.mult).then_inc(ck_raw, 1)
            for c in range(MC):
                dve.wait_ge(cv_ps, c + 1)
                V.tensor_scalar(cv[:, c, :], psum[6 + c][:, 0:M], rmem[:, c:c + 1], None,
                                ALU.mult).then_inc(dve_chain, 1)
                links[0] += 1
            for d in range(KD):
                x_low(0, S_G1, d)
            dve.wait_ge(ck_stat, 1)
            mean(1, psum[3][:, 0:4 * MC], msq_[:, 0:4 * MC], 1.0 / DH)
            rsqrt(1, 4 * MC, rmk[:].rearrange("p j c e -> p (j c e)"), rmk_ready)
            dve.wait_ge(ckbc_ps, 1)
            dve.wait_ge(ck_raw, 2)
            V.scalar_tensor_tensor(out=ck[:].rearrange("p j t -> p (j t)"), in0=psum[2][:], scalar=gain_qk[:, 1:2],
                                   in1=ck[:].rearrange("p j t -> p (j t)"), op0=ALU.mult,
                                   op1=ALU.mult).then_inc(ck_ready, 1)
            dve.wait_ge(ab_hi, 1)
            V.tensor_tensor(ablo[:], abr[:], abhi[:].bitcast(F32), ALU.subtract).then_inc(ab_lo, 1)

            def ffn_hidden(n_of):
                for a in range(2):
                    dve.wait_ge(gate_done, n_of(a) + 1)
                    if not (isinstance(n_of(a), int) and n_of(a) < 2):
                        dve.wait_ge(h_hi, n_of(a) + (-1))
                        dve.wait_ge(h_lo, n_of(a) + (-1))
                    V.tensor_tensor(gbuf[:, a, :], psum[a][:], rbc[:], ALU.mult).then_inc(gate_scaled, 1)
                for a in range(2):
                    dve.wait_ge(silu_done, n_of(a) + 1)
                    V.tensor_tensor(gbuf[:, a, :], gbuf[:, a, :], rbc[:], ALU.mult).then_inc(silu_scaled, 1)
                for a in range(2):
                    dve.wait_ge(up_done, n_of(a) + 1)
                    dve.wait_ge(silu_scaled, n_of(a) + 1)
                    V.tensor_tensor(gbuf[:, a, :], psum[2 + a][:], gbuf[:, a, :], ALU.mult).then_inc(h_done, 1)

            def ffn_low(n_of, b):
                for a in range(2):
                    dve.wait_ge(h_hi, n_of(a) + 1)
                    V.tensor_tensor(hlo[:, 2 * b + a, :], gbuf[:, a, :], hhi[:, 2 * b + a, :].bitcast(F32),
                                    ALU.subtract).then_inc(h_lo, 1)

            def ffn_add(before, d):
                dve.wait_ge(down_done, before + (d + 1))
                V.scalar_tensor_tensor(out=x[:, d, :], in0=psum[4 + d % 4][:], scalar=0.5, in1=x[:, d, :],
                                       op0=ALU.mult, op1=ALU.add).then_inc(x_added, 1)

            def ffn(f):
                n0, d0 = 2 * FG * f, KD * FG * f
                ffn_hidden(lambda a: n0 + a)
                ffn_low(lambda a: n0 + a, 0)
                with dve.Fori(0, FG // 2) as j:
                    for b in range(2):
                        n_of = lambda a, b=b: 4 * j + (n0 + 2 * (b + 1) + a)
                        ffn_hidden(n_of)
                        ffn_low(n_of, 1 - b)
                        dve.wait_ge(gate_scaled, 4 * j + (n0 + 2 * b + 4))
                        for d in range(KD):
                            ffn_add(2 * KD * j + (d0 + KD * b), d)
                dve.wait_ge(x_added, d0 + KD * (FG - 1))

            x_stat(0, 2)
            ffn(0)
            for d in range(KD):
                ffn_add(KD * (FG - 1), d)
                if d >= 1:
                    x_low(1, S_GM, d - 1)
            x_low(1, S_GM, KD - 1)

            V.memset(cin[:, :, 0:3], 0.0).then_inc(dve_chain, 1)
            links[0] += 1
            x_stat(1, 3)
            dve.wait_ge(dve_chain, links[0])

            def evacuate(q, dst):
                dve.wait_ge(p_done, q + 1)
                V.tensor_tensor(dst, psum[q % 4][:], rbc[:], ALU.mult).then_inc(p_evac, 1)

            def conv(q):
                o, i = cout[:, q % 2, :], cin[:, q % 2, :]
                dve.wait_ge(p_evac, q + 1)
                if q >= 2:
                    dve.wait_ge(qkv_ready, q - 1)
                w = S_CONV + 4 * q
                link(V.tensor_scalar(o, i[:, 0:T], col(w), None, ALU.mult))
                for j in (1, 2):
                    link(V.scalar_tensor_tensor(out=o, in0=i[:, j:j + T], scalar=col(w + j), in1=o,
                                                op0=ALU.mult, op1=ALU.add))
                V.scalar_tensor_tensor(out=o, in0=i[:, 3:3 + T], scalar=col(w + 3), in1=o,
                                       op0=ALU.mult, op1=ALU.add).then_inc(conv_done, 1)

            for q in range(12):
                if q >= 2:
                    dve.wait_ge(conv_done, q - 1)
                evacuate(q, cin[:, q % 2, 3:3 + T])
                conv(q)
            dve.wait_ge(ab_ps, 1)
            V.tensor_copy(abt[:, :], psum[6][0:8, :]).then_inc(ab_sb, 1)
            dve.wait_ge(sqk_used, 8)
            mean(4, psum[7][:, 0:32], msq_[:, 0:32], 1.0)
            for q in range(12, 14):
                evacuate(q, z[:, q - 12, :])
            dve.wait_ge(ab_tm, 1)
            abv = psum[6][:, 0:32].rearrange("p (c n) -> p c n", c=NC_)
            for c in range(NC_):
                V.scalar_tensor_tensor(out=gate_hc(G_A)[:, :, c], in0=abv[:, c, 0:H], scalar=rtm[:, 1, c:c + 1],
                                       in1=small[:, S_DT:S_DT + H], op0=ALU.mult, op1=ALU.add).then_inc(dve_chain, 1)
                V.tensor_scalar(gate_hc(G_B)[:, :, c], abv[:, c, H:2 * H], rtm[:, 1, c:c + 1], None,
                                ALU.mult).then_inc(dve_chain, 1)
                links[0] += 2
            dve.wait_ge(dve_chain, links[0])
            V.scalar_tensor_tensor(out=gate(G_NEG), in0=gate(G_A), scalar=-1.0, in1=gate(G_A), op0=ALU.mult,
                                   op1=ALU.min).then_inc(g_dve, 1)
            for q in range(14, 16):
                evacuate(q, z[:, q - 12, :])
            rsqrt(4, 32, rqk[:].rearrange("p t c -> p (t c)"), rqk_ready)
            dve.wait_ge(g_act, 1)
            V.tensor_scalar(gate(G_EXP), gate(G_EXP), 1.0, None, ALU.add).then_inc(g_dve, 1)
            dve.wait_ge(g_act, 2)
            link(V.tensor_scalar(gate(G_EB), gate(G_EB), 1.0, None, ALU.add))
            link(V.reciprocal(gate(G_BETA), gate(G_EB)))
            for q in range(16, 18):
                if q == 16:
                    dve.wait_ge(conv_done, 12)
                evacuate(q, mq[:, q - 16, :])
            dve.wait_ge(g_act, 4)
            link(V.scalar_tensor_tensor(out=gate(G_LN), in0=gate(G_A), scalar=0.0, in1=gate(G_LN), op0=ALU.max,
                                        op1=ALU.add))
            V.scalar_tensor_tensor(out=gate_hc(G_G), in0=gate_hc(G_LN), scalar=-1.0,
                                   in1=rowmax[:].unsqueeze(2).broadcast_to([P, H, NC_]), op0=ALU.mult,
                                   op1=ALU.mult).then_inc(g_dve, 1)
            dve.wait_ge(g_pe, 1)
            link(V.tensor_copy(gates[:, G_GC:G_GC + 2, :], psum[6][:, 64:96].rearrange("p (n m) -> p n m", n=2)))
            V.tensor_tensor(gate(G_GT), gate(G_GL), gate(G_GC), ALU.subtract).then_inc(g_dve, 1)
            for q in range(18, 22):
                evacuate(q, (mk, cq)[(q - 18) // 2][:, q % 2, :])
            dve.wait_ge(g_act, 5)
            dve.wait_ge(rqk_ready, 1)
            rq = rqk[:, 0:H, :].rearrange("p h c -> p (h c)")
            rk = rqk[:, H:2 * H, :].rearrange("p h c -> p (h c)")
            link(V.tensor_tensor(gates[:, G_RKB, :], rk, gates[:, G_BETA, :], ALU.mult))
            link(V.scalar_tensor_tensor(out=gate(G_SR), in0=gate(G_RKB), scalar=-1.0, in1=gate(G_EG), op0=ALU.mult,
                                        op1=ALU.mult))
            link(V.tensor_tensor(gates[:, G_ET, :], rk, gates[:, G_ET, :], ALU.mult))
            V.tensor_scalar(rq, rq, float(P) ** -0.5, None, ALU.mult).then_inc(gates_ready, 1)
            for c in range(NC_):
                dve.wait_ge(p_done, 22 + c + 1)
                V.tensor_scalar(mv[:, c, :], psum[(22 + c) % 4][:, 0:M], rtm[:, 1, c:c + 1], None,
                                ALU.mult).then_inc(p_evac, 1)
            dve.wait_ge(sqa_used, 6)
            mean(5, psum[7][:, 0:48], msq_[:, 0:48], 1.0 / DH)
            rsqrt(5, 48, ratt[:].rearrange("p t c e -> p (t c e)"), ratt_ready)
            dve.wait_ge(ratt_ready, 1)
            for h in range(H):
                for t0, s in ((0, SCALE / SLOPES[h]), (4, SCALE)):
                    r = ratt[:, t0 + h // 2, :, h % 2]
                    link(V.tensor_scalar(r, r, s, None, ALU.mult))

            def prep(c):
                dve.wait_ge(egb_ready, c + 1)
                if c >= 1:
                    dve.wait_ge(at_ready, 4 * c)
                    dve.wait_ge(pt_ready, 4 * c)
                for h in range(H):
                    i = V.scalar_tensor_tensor(out=dec[:, h, :], in0=heads(0)[:, h, :], scalar=gcol(G_GC, h, c),
                                               in1=negmask, op0=ALU.subtract, op1=ALU.add)
                i.then_inc(dpre, 1)
                dve.wait_ge(prep_ps[3], c + 1)
                V.tensor_tensor(qkv[:, 0:H, c * P:(c + 1) * P], qkv[:, 0:H, c * P:(c + 1) * P], egb[:],
                                ALU.mult).then_inc(egb_used, 1)
                dve.wait_ge(prep_ps[1], c + 1)
                dve.wait_ge(dexp, c + 1)
                if c >= 2:
                    dve.wait_ge(b_ready, (c // 2) * 2 * LEVELS)
                V.tensor_tensor(at_[:, c % 2, :, :], heads(1), dec[:], ALU.mult).then_inc(rb_read, 1)
                dve.wait_ge(rb_read, c + 1)
                for h in range(H):
                    V.scalar_tensor_tensor(out=at_[:, c % 2, h, :], in0=heads(2)[:, h, :],
                                           scalar=rqk[:, H + h, c:c + 1], in1=at_[:, c % 2, h, :],
                                           op0=ALU.mult, op1=ALU.mult).then_inc(at_ready, 1)
                for h in range(H):
                    V.scalar_tensor_tensor(out=pt[:, c, h, :], in0=heads(3)[:, h, :],
                                           scalar=rqk[:, H + h, c:c + 1], in1=dec[:, h, :],
                                           op0=ALU.mult, op1=ALU.mult).then_inc(pt_ready, 1)
                dve.wait_ge(prep_ps[5], c + 1)
                for h in range(H):
                    V.tensor_scalar(qkv[:, 8 + h, c * P:(c + 1) * P], heads(1)[:, h, :], gcol(G_BETA, h, c), None,
                                    ALU.mult).then_inc(bv_ready, 1)

            def mask_level(pair, l, j):
                n = pair * 2 * LEVELS + l * 2 + j
                if l >= 1:
                    if l == 1:
                        dve.wait_ge(xp_ps, pair * 2 * (LEVELS - 1) + j + 1)
                        dve.wait_ge(xt_upd, n - 1)
                    else:
                        dve.wait_ge(y_ps, pair * 2 * (LEVELS - 1) + (l - 2) * 2 + j + 1)
                else:
                    dve.wait_ge(at_ready, 4 * (2 * pair + j + 1))
                V.tensor_tensor(bm[:, j, :, :], at_[:, j, :, :], over_heads(level(l)), ALU.mult).then_inc(b_ready, 1)

            def inverse(pair):
                for j in range(2):
                    mask_level(pair, 0, j)
                for l in range(LEVELS):
                    for j in range(2):
                        n = pair * 2 * LEVELS + l * 2 + j
                        c = 2 * pair + j
                        xt_c, xn_j = xt[:, c, :, :], xn[:, j, :, :]
                        if l == 0:
                            dve.wait_ge(b_ready, n + 1)
                            V.tensor_tensor(xt_c, over_heads(ident), bm[:, j, :, :], ALU.subtract).then_inc(xt_upd, 1)
                            dve.wait_ge(xp_ps, pair * 2 * (LEVELS - 1) + j + 1)
                            V.tensor_tensor(xn_j, over_heads(ident), heads(5 + 2 * j), ALU.subtract).then_inc(x_upd, 1)
                            mask_level(pair, 1, j)
                            continue
                        if l + 1 < LEVELS:
                            mask_level(pair, l + 1, j)
                            m = pair * 2 * (LEVELS - 1) + l * 2 + j
                            dve.wait_ge(xp_ps, m + 1)
                            dve.wait_ge(x_upd, m - 1)
                            V.tensor_tensor(xn_j, xn_j, heads(5 + 2 * j), ALU.subtract).then_inc(x_upd, 1)
                        dve.wait_ge(xtp_ps, pair * 2 * (LEVELS - 1) + (l - 1) * 2 + j + 1)
                        dve.wait_ge(xt_upd, n - 1)
                        V.tensor_tensor(xt_c, xt_c, heads(4 + 2 * j), ALU.subtract).then_inc(xt_upd, 1)

            for pair in range(2):
                prep(2 * pair)
                prep(2 * pair + 1)
                if pair == 0:
                    for t in range(2):
                        dve.wait_ge(mkbc_ps, t + 1)
                        V.scalar_tensor_tensor(out=mk[:, t, :], in0=psum[2 + t][:], scalar=gain_qk[:, 0:1],
                                               in1=mk[:, t, :], op0=ALU.mult, op1=ALU.mult).then_inc(mk_ready, 1)
                inverse(pair)

            for a in range(NJ + 3):
                if a < NJ:
                    kind, h, c = jobs[a]
                    m4 = slice(a % 4, a % 4 + 1)
                    dve.wait_ge(s_ps, a + 1)
                    if a >= 2:
                        dve.wait_ge(exp_done, a - 1)
                    if kind == "moba":
                        w = P * (c + 1)
                        r = ratt[:, h // 2, c, h % 2:h % 2 + 1]
                        rel = cst[:, C_REL + T - w:C_REL + T]
                        link(V.scalar_tensor_tensor(out=sc[:, a % 2, 0:w], in0=psum[4 + a % 2][:, 0:w], scalar=r,
                                                    in1=rel, op0=ALU.mult, op1=ALU.add))
                        link(V.tensor_reduce(rowmax[:, m4], sc[:, a % 2, 0:w], AX.X, ALU.max))
                        V.tensor_scalar(negmax[:, m4], rowmax[:, m4], -SLOPES[h], None, ALU.mult).then_inc(nm_ready, 1)
                    else:
                        r = ratt[:, 4 + h // 2, c, h % 2:h % 2 + 1]
                        link(V.tensor_reduce(rowmax[:, m4], psum[4 + a % 2][:, 0:M], AX.X, ALU.max))
                        V.tensor_scalar(negmax[:, m4], rowmax[:, m4], r, -1.0, ALU.mult,
                                        ALU.mult).then_inc(nm_ready, 1)
                if 1 <= a < NJ + 1:
                    kind, h, c = jobs[a - 1]
                    w = P * (c + 1) if kind == "moba" else M
                    m4 = slice((a - 1) % 4, (a - 1) % 4 + 1)
                    dve.wait_ge(exp_done, a)
                    link(V.reciprocal(rowinv[:, m4], rowsum[:, m4]))
                    pr = prob[:, (a - 1) % 3, 0:w]
                    V.tensor_scalar(pr, pr, rowinv[:, m4], None, ALU.mult).then_inc(p_norm, 1)
                c, s = a // JC, a % JC
                if c < NC_ and s == 0 and c >= 1:
                    dve.wait_ge(ks_ps, c)
                    if c >= 2:
                        dve.wait_ge(v_ps, c)
                    for h in range(H):
                        V.scalar_tensor_tensor(out=rsb[:, h, :], in0=heads(0)[:, h, :], scalar=gcol(G_SR, h, c),
                                               in1=qkv[:, 8 + h, c * P:(c + 1) * P], op0=ALU.mult,
                                               op1=ALU.add).then_inc(r_sb, 1)
                if c < NC_ - 1 and s == 2:
                    dve.wait_ge(kv_ps, c + 1)
                    if c == 0:
                        V.tensor_copy(state[:, 1, :, :], heads(3)).then_inc(s_upd, 4)
                    else:
                        for h in range(H):
                            V.scalar_tensor_tensor(out=state[:, (c + 1) % 2, h, :], in0=state[:, c % 2, h, :],
                                                   scalar=gcol(G_EGL, h, c), in1=heads(3)[:, h, :],
                                                   op0=ALU.mult, op1=ALU.add).then_inc(s_upd, 1)
                if a >= JC + 2 and (a - 2) % JC == 0:
                    c = (a - 2) // JC - 1
                    dve.wait_ge(yb_hi, c + 1)
                    V.tensor_tensor(alo[:, 4:8, c * P:(c + 1) * P], heads(7),
                                    ahi[:, 4:8, c * P:(c + 1) * P].bitcast(F32), ALU.subtract).then_inc(yb_lo, 1)

            dve.wait_ge(o_stat, 1)
            link(V.tensor_tensor(inv0[:, 0:16], rq, rq, ALU.mult))
            link(V.scalar_tensor_tensor(out=newt[:, 0:16], in0=psum[0][:, 0:16], scalar=1.0 / P, in1=inv0[:, 0:16],
                                        op0=ALU.mult, op1=ALU.mult))
            mean(6, newt[:, 0:16], msq_[:, 0:16], 1.0)
            rsqrt(6, 16, gates[:, G_A, :], dve_chain)
            links[0] += 1
            dve.wait_ge(dve_chain, links[0])
            V.tensor_tensor(gates[:, G_B, :], gates[:, G_A, :], rq, ALU.mult).then_inc(ro_ready, 1)
            for h in range(H):
                yv = qkv[:, 8 + h, :]
                dve.wait_ge(obc_ps, h + 1)
                link(V.scalar_tensor_tensor(out=yv, in0=psum[h][:], scalar=col(S_OG), in1=qkv[:, h, :],
                                            op0=ALU.mult, op1=ALU.mult))
                V.tensor_tensor(yv, yv, z[:, h, :], ALU.mult).then_inc(y_tm, 1)
                if h >= 1:
                    dve.wait_ge(y_hi, h)
                    V.tensor_tensor(alo[:, h - 1, :], qkv[:, 7 + h, :], ahi[:, h - 1, :].bitcast(F32),
                                    ALU.subtract).then_inc(y_lo, 1)
            dve.wait_ge(y_hi, H)
            V.tensor_tensor(alo[:, H - 1, :], qkv[:, 11, :], ahi[:, H - 1, :].bitcast(F32),
                            ALU.subtract).then_inc(y_lo, 1)
            for d in range(KD):
                dve.wait_ge(wo_ps, d + 1)
                V.tensor_tensor(x[:, d, :], x[:, d, :], psum[4 + d % 4][:], ALU.add).then_inc(xo_added, 1)
            for d in range(KD):
                x_low(2, S_G2, d)
            x_stat(2, 7)
            ffn(1)
            for d in range(KD):
                ffn_add(KD * (2 * FG - 1), d)

        @block.tensor
        def _(pe):
            E = nc.tensor

            def split_product(dst, w, act_, n, last, flip=False, used=False):
                terms = ((w[0], act_[0]), (w[0], act_[1]), (w[1], act_[0]))
                if flip:
                    terms = tuple((b, a) for a, b in terms)
                for i, (a, b) in enumerate(terms):
                    ins = E.matmul(dst, a, b, start=(n == 0 and i == 0), stop=(n == last and i == 2))
                    if used and i == 0:
                        ins.then_inc(w_used, 1)
                return ins

            def wparts(u, k, c0, n, width):
                return wslice(whi, u, k, c0, n, width), wslice(wlo, u, k, c0, n, width)

            def x_stats(stage):
                pe.wait_ge(sq_ready, KD * (stage + 1))
                for d in range(KD):
                    for c in range(NC_):
                        i = E.matmul(psum[4][:, c:c + 1], sqx[:, d, c * P:(c + 1) * P], ones[:, 0:1],
                                     start=(d == 0 and c == 0), stop=(d == KD - 1 and c == NC_ - 1),
                                     skip_group_check=True)
                        if d == 0 and c == 0:
                            i.then_inc(w_used, 1)
                i.then_inc(stat_done, 1)

            def spread(bank, c0, column):
                return E.matmul(psum[bank][:, c0:c0 + P], column, ident, start=True, stop=True)

            def spread_pair(bank, c0, two):
                for e in range(2):
                    i = E.matmul(psum[bank][e * DH:(e + 1) * DH, c0:c0 + P], two[:, e:e + 1].broadcast_to([P, DH]),
                                 ident, start=True, stop=True)
                return i

            def x_spread(stage):
                pe.wait_ge(rtm_ready, stage + 1)
                for c in range(NC_):
                    i = spread(5, c * P, rtm[:, stage, c:c + 1].broadcast_to([P, P]))
                i.then_inc(rbc_ps, 1)

            pe.wait_ge(w_lo, 1)
            for j in range(2):
                for k in range(KD):
                    if j == 0:
                        pe.wait_ge(mem_lo, k + 1)
                    i = split_product(psum[j][:, 0:M], wparts(0, k, j * P, P, 256),
                                      (memhi[:, k, :], memlo[:, k, :]), k, KD - 1)
                i.then_inc(ck_ps, 1)
            pe.wait_ge(cst_in, 16)
            pe.wait_ge(mem_sq, 1)
            for k in range(KD):
                for c in range(MC):
                    i = E.matmul(psum[4][:, c:c + 1], memsq[:, k, c * P:(c + 1) * P], ones[:, 0:1],
                                 start=(k == 0 and c == 0), stop=(k == KD - 1 and c == MC - 1),
                                 skip_group_check=True)
                    if k == 0 and c == 0:
                        i.then_inc(w_used, 1)
            i.then_inc(mem_stat, 1)
            pe.wait_ge(w_lo, 2)
            for c in range(MC):
                for k in range(KD):
                    i = split_product(psum[6 + c][:, 0:M], wparts(1, k, 0, M, 256),
                                      (memhi[:, k, c * P:(c + 1) * P], memlo[:, k, c * P:(c + 1) * P]),
                                      k, KD - 1, flip=True)
                i.then_inc(cv_ps, 1)
            pe.wait_ge(rm_ready, 1)
            for c in range(MC):
                i = spread(2, c * P, rmem[:, c:c + 1].broadcast_to([P, P]))
                if c == 0:
                    i.then_inc(w_used, 1)
            i.then_inc(rmbc_ps, 1)
            pe.wait_ge(ck_sq, 1)
            for j in range(2):
                for c in range(MC):
                    n = 2 * (j * MC + c)
                    i = E.matmul(psum[3][:, n:n + 2], mksq[:, j, c * P:(c + 1) * P], headsel, start=True, stop=True)
            i.then_inc(ck_stat, 1)
            pe.wait_ge(rmk_ready, 1)
            for j in range(2):
                for c in range(MC):
                    i = spread_pair(2, j * M + c * P, rmk[:, j, c, :])
            i.then_inc(ckbc_ps, 1)

            def up_tile(u, a, bank, done, free=None, used=False):
                if free is not None:
                    pe.wait_ge(*free)
                for k in range(KD):
                    i = split_product(psum[bank][:], wparts(u, k, a * P, P, 256),
                                      (ahi[:, k, :], alo[:, k, :]), k, KD - 1, used=used and k == 0)
                return i.then_inc(done, 1)

            def down(u, b, free):
                for d in range(KD):
                    if d >= 4:
                        pe.wait_ge(x_added, free + (d - 3))
                    for k in range(2):
                        i = split_product(psum[4 + d % 4][:], wparts(u, k, d * P, P, D),
                                          (hhi[:, 2 * b + k, :], hlo[:, 2 * b + k, :]), k, 1,
                                          used=d == 0 and k == 0)
                    i.then_inc(down_done, 1)

            def ffn(f, stage):
                n0, u0, d0 = 2 * FG * f, U_FFN[f], KD * FG * f
                pe.wait_ge(w_lo, u0 + 1)
                for k in range(KD):
                    pe.wait_ge(a_lo, KD * stage + k + 1)
                    i = split_product(psum[0][:], wparts(u0, k, 0, P, 256), (ahi[:, k, :], alo[:, k, :]), k, KD - 1,
                                      used=f == 1 and k == 0)
                i.then_inc(gate_done, 1)
                up_tile(u0, 1, 1, gate_done)
                x_stats(stage)
                pe.wait_ge(w_lo, u0 + 2)
                if f == 0:
                    pe.wait_ge(ck_ready, 1)
                up_tile(u0 + 1, 0, 2, up_done)
                x_spread(stage)
                up_tile(u0 + 1, 1, 3, up_done)
                with pe.Fori(0, FG // 2) as j:
                    for b in range(2):
                        v = u0 + 2 + 3 * b
                        pe.wait_ge(w_lo, 6 * j + (v + 1))
                        for a in range(2):
                            up_tile(v, a, a, gate_done, (gate_scaled, 4 * j + (n0 + 2 * b + a + 1)), a == 0)
                        pe.wait_ge(w_lo, 6 * j + (v + 2))
                        for a in range(2):
                            up_tile(v + 1, a, 2 + a, up_done, (h_done, 4 * j + (n0 + 2 * b + a + 1)), a == 0)
                        pe.wait_ge(w_lo, 6 * j + (v + 3))
                        pe.wait_ge(h_lo, 4 * j + (n0 + 2 * b + 2))
                        pe.wait_ge(gate_scaled, 4 * j + (n0 + 2 * b + 4))
                        down(v + 2, b, 2 * KD * j + (d0 + KD * b))
                pe.wait_ge(w_lo, u0 + 3 * FG)
                pe.wait_ge(h_lo, n0 + 2 * FG)
                pe.wait_ge(x_added, d0 + KD * (FG - 1))
                down(u0 + 3 * FG - 1, 0, d0 + KD * (FG - 1))

            ffn(0, 0)

            def in_tile(q, n, a):
                if q >= 4:
                    pe.wait_ge(p_evac, q - 3)
                up_tile(U_IN + n, a, q % 4, p_done, used=n >= 2 and a == 0)

            for n in range(12):
                pe.wait_ge(w_lo, U_IN + n + 1)
                if n == 0:
                    for k in range(KD):
                        pe.wait_ge(a_lo, KD + k + 1)
                        i = split_product(psum[0][:], wparts(U_IN, k, 0, P, 256), (ahi[:, k, :], alo[:, k, :]),
                                          k, KD - 1, used=k == 0)
                    i.then_inc(p_done, 1)
                    in_tile(1, 0, 1)
                elif n == 11:
                    for c in range(NC_):
                        pe.wait_ge(p_evac, 22 + c - 3)
                        for k in range(KD):
                            i = split_product(psum[(22 + c) % 4][:, 0:M], wparts(U_IN + n, k, 0, M, 256),
                                              (ahi[:, k, c * P:(c + 1) * P], alo[:, k, c * P:(c + 1) * P]),
                                              k, KD - 1, flip=True, used=c == 0 and k == 0)
                        i.then_inc(p_done, 1)
                else:
                    in_tile(2 * n, n, 0)
                    if n == 1:
                        x_spread(1)
                    in_tile(2 * n + 1, n, 1)
                if n == 0:
                    x_stats(1)
                if 2 <= n < 6:
                    for t in (2 * n - 4, 2 * n - 3):
                        pe.wait_ge(sqk_ready, t + 1)
                        for c in range(NC_):
                            m = t * NC_ + c
                            i = E.matmul(psum[7][:, m:m + 1], sqk[:, t % 4, c * P:(c + 1) * P], ones[:, 0:1],
                                         start=True, stop=True)
                        i.then_inc(sqk_used, 1)
                if n == 5:
                    pe.wait_ge(ab_lo, 1)
                    for k in range(KD):
                        i = split_product(psum[6][0:8, :], (abhi[:, k, :], ablo[:, k, :]),
                                          (ahi[:, k, :], alo[:, k, :]), k, KD - 1)
                    i.then_inc(ab_ps, 1)
                if n == 6:
                    pe.wait_ge(ab_sb, 1)
                    for c in range(NC_):
                        i = E.matmul(psum[6][:, 8 * c:8 * c + 8], abt[:, c * P:(c + 1) * P], ident[0:8, 0:8],
                                     is_transpose=True, start=True, stop=True)
                    i.then_inc(ab_tm, 1)
                if n == 8:
                    pe.wait_ge(g_dve, 3)
                    E.matmul(psum[6][:, 64:80], upper, gates[:, G_G, :], start=True, stop=True)
                    E.matmul(psum[6][:, 80:96], ones, gates[:, G_G, :], start=True, stop=True).then_inc(g_pe, 1)
                if n >= 9:
                    for t in (2 * n - 18, 2 * n - 17):
                        pe.wait_ge(sqa_ready, t + 1)
                        if t == 0:
                            pe.wait_ge(rqk_ready, 1)
                        for c in range(NC_):
                            m = 2 * (t * NC_ + c)
                            i = E.matmul(psum[7][:, m:m + 2], sqa[:, t, c * P:(c + 1) * P], headsel,
                                         start=True, stop=True)
                            if n == 11 and t == 4 and c == 0:
                                i.then_inc(w_used, 1)
                        i.then_inc(sqa_used, 1)

            def prep(c):
                cs = slice(c * P, (c + 1) * P)
                if c == 0:
                    pe.wait_ge(gates_ready, 1)
                    pe.wait_ge(p_evac, 26)
                    pe.wait_ge(qkv_ready, 12)
                else:
                    pe.wait_ge(kt_ready, 4 * c)
                    pe.wait_ge(bv_ready, 4 * c)
                    pe.wait_ge(at_ready, 4 * c)
                    pe.wait_ge(pt_ready, 4 * c)
                    if c == 2:
                        pe.wait_ge(mk_ready, 2)
                for h in range(H):
                    i = E.matmul(heads(0)[:, h, :], gcol(G_G, h, c).broadcast_to([P, P]), upper, start=True, stop=True)
                i.then_inc(prep_ps[0], 1)
                for h in range(H):
                    i = E.matmul(heads(1)[:, h, :], gcol(G_RKB, h, c).broadcast_to([P, P]), ident,
                                 start=True, stop=True)
                i.then_inc(prep_ps[1], 1)
                for h in range(H):
                    i = E.matmul(heads(2)[:, h, :], qkv[:, 4 + h, cs], qkv[:, 4 + h, cs], start=True, stop=True)
                i.then_inc(prep_ps[2], 1)
                for h in range(H):
                    i = E.matmul(heads(3)[:, h, :], qkv[:, 4 + h, cs], qkv[:, h, cs], start=True, stop=True)
                i.then_inc(prep_ps[3], 1)
                pe.wait_ge(dpre, c + 1)
                pe.wait_ge(egb_ready, c + 1)
                for h in range(H):
                    i = E.transpose(heads(0)[:, h, :], qkv[:, 4 + h, cs], ident)
                i.then_inc(prep_ps[4], 1)
                pe.wait_ge(rb_read, c + 1)
                for h in range(H):
                    i = E.transpose(heads(1)[:, h, :], qkv[:, 8 + h, cs], ident)
                i.then_inc(prep_ps[5], 1)

            def inverse(pair):
                for l in range(LEVELS):
                    for j in range(2):
                        n = pair * 2 * LEVELS + l * 2 + j
                        m = pair * 2 * (LEVELS - 1) + l * 2 + j
                        c = 2 * pair + j
                        pe.wait_ge(b_ready, n + 1)
                        if l == 0:
                            for h in range(H):
                                i = E.matmul(heads(5 + 2 * j)[:, h, :], bm[:, j, h, :], ident, start=True, stop=True)
                            i.then_inc(xp_ps, 1)
                            continue
                        pe.wait_ge(x_upd, pair * 2 * (LEVELS - 1) + (l - 1) * 2 + j + 1)
                        pe.wait_ge(xt_upd, n - 1)
                        for h in range(H):
                            i = E.matmul(heads(4 + 2 * j)[:, h, :], bm[:, j, h, :], xn[:, j, h, :],
                                         start=True, stop=True)
                        i.then_inc(y_ps, 1)
                    if l == 0:
                        continue
                    for j in range(2):
                        m = pair * 2 * (LEVELS - 1) + (l - 1) * 2 + j
                        c = 2 * pair + j
                        pe.wait_ge(y_sb, m + 1)
                        if l + 1 < LEVELS:
                            for h in range(H):
                                i = E.matmul(heads(5 + 2 * j)[:, h, :], xt[:, c, h, :], ysb[:, j, h, :],
                                             start=True, stop=True)
                            i.then_inc(xp_ps, 1)
                        for h in range(H):
                            i = E.matmul(heads(4 + 2 * j)[:, h, :], ysb[:, j, h, :], xt[:, c, h, :],
                                         start=True, stop=True)
                        i.then_inc(xtp_ps, 1)

            for pair in range(2):
                prep(2 * pair)
                prep(2 * pair + 1)
                if pair == 0:
                    pe.wait_ge(ratt_ready, 1)
                    pe.wait_ge(at_ready, 8)
                    pe.wait_ge(pt_ready, 8)
                    for t in range(2):
                        for c in range(NC_):
                            i = spread_pair(2 + t, c * P, ratt[:, 2 + t, c, :])
                        i.then_inc(mkbc_ps, 1)
                inverse(pair)

            pe.wait_ge(xt_upd, 4 * LEVELS)
            pe.wait_ge(bv_ready, 16)
            pe.wait_ge(kt_ready, 16)
            pe.wait_ge(pt_ready, 16)
            pe.wait_ge(egb_used, 4)
            for a in range(NJ + 3):
                if a < NJ:
                    kind, h, c = jobs[a]
                    if a >= 2:
                        if jobs[a - 2][0] == "moba":
                            pe.wait_ge(nm_ready, a - 1)
                        else:
                            pe.wait_ge(exp_done, a - 1)
                    r = slice(DH * (h % 2), DH * (h % 2) + DH)
                    cs = slice(c * P, (c + 1) * P)
                    if kind == "moba":
                        w = P * (c + 1)
                        E.matmul(psum[4 + a % 2][:, 0:w], mq[r, h // 2, cs], mk[r, h // 2, 0:w], start=True,
                                 stop=True).then_inc(s_ps, 1)
                    else:
                        E.matmul(psum[4 + a % 2][:, 0:M], cq[r, h // 2, cs], ck[r, h // 2, :], start=True,
                                 stop=True).then_inc(s_ps, 1)
                c, s = a // JC, a % JC
                if c < NC_:
                    cs = slice(c * P, (c + 1) * P)
                    if s == 0 and c >= 1:
                        pe.wait_ge(s_upd, 4 * c)
                        for h in range(H):
                            i = E.matmul(heads(0)[:, h, :], qkv[:, 4 + h, cs], state[:, c % 2, h, :],
                                         start=True, stop=True)
                        i.then_inc(ks_ps, 1)
                    if s == 1:
                        if c >= 1:
                            pe.wait_ge(r_sb, 4 * c)
                        for h in range(H):
                            rhs = rsb[:, h, :] if c >= 1 else qkv[:, 8 + h, cs]
                            i = E.matmul(heads(1)[:, h, :], xt[:, c, h, :], rhs, start=True, stop=True)
                        i.then_inc(v_ps, 1)
                    if s == 2:
                        pe.wait_ge(v_sb, c + 1)
                        for h in range(H):
                            i = E.matmul(heads(3)[:, h, :], kt[:, c, h, :], vsb[:, h, :], start=True, stop=True)
                        i.then_inc(kv_ps, 1)
                        for h in range(H):
                            if c >= 1:
                                E.matmul(heads(2)[:, h, :], state[:, c % 2, h, :], qkv[:, h, cs], start=True,
                                         stop=False)
                            i = E.matmul(heads(2)[:, h, :], vsb[:, h, :], pt[:, c, h, :], start=(c == 0), stop=True)
                        i.then_inc(o_ps, 1)
                if 2 <= a < NJ + 2:
                    kind, h, c = jobs[a - 2]
                    n = c + 1 if kind == "moba" else MC
                    pe.wait_ge(p_norm, a - 1)
                    if a >= 3:
                        pe.wait_ge(pt_sb, a - 2)
                    for b in range(n):
                        i = E.transpose(heads(6)[:, b, :], prob[:, (a - 2) % 3, b * P:(b + 1) * P], ident)
                    i.then_inc(pt_ps, 1)
                if a >= 3:
                    kind, h, c = jobs[a - 3]
                    n = c + 1 if kind == "moba" else MC
                    val = mv if kind == "moba" else cv
                    t = h // 2 + (0 if kind == "moba" else 2)
                    pe.wait_ge(pt_sb, a - 2)
                    if (a - 3) % JC == 0 and c >= 1:
                        pe.wait_ge(yb_lo, c)
                    dst = heads(7)[DH * (h % 2):DH * (h % 2) + DH, t, :]
                    for b in range(n):
                        i = E.matmul(dst, val[:, b, h * DH:(h + 1) * DH], ptr[:, (a - 1) % 2, b, :],
                                     start=(b == 0), stop=(b == n - 1))
                    i.then_inc(pv_done, 1)
            pe.wait_ge(o_sb, 8)
            for h in range(H):
                for c in range(NC_):
                    m = h * NC_ + c
                    i = E.matmul(psum[0][:, m:m + 1], qkv[:, H + h, c * P:(c + 1) * P], ones[:, 0:1],
                                 start=True, stop=True)
            i.then_inc(o_stat, 1)

            order = [4, 5, 6, 7, 0, 1, 2, 3]

            def out_terms(d, ks):
                for k in ks:
                    i = split_product(psum[4 + d % 4][:], wparts(U_OUT + d // 2, k, (d % 2) * P, P, 256),
                                      (ahi[:, k, :], alo[:, k, :]), order.index(k), KD - 1,
                                      used=d >= 2 and d % 2 == 0 and k == order[0])
                return i

            pe.wait_ge(w_lo, U_OUT + 1)
            pe.wait_ge(yb_lo, NC_)
            for d in (0, 1):
                out_terms(d, order[:4])
            pe.wait_ge(ro_ready, 1)
            for h in range(H):
                for c in range(NC_):
                    i = spread(h, c * P, gcol(G_B, h, c).broadcast_to([P, P]))
                i.then_inc(obc_ps, 1)
            for d in (0, 1):
                for k in order[4:]:
                    pe.wait_ge(y_lo, k + 1)
                    i = out_terms(d, [k])
                i.then_inc(wo_ps, 1)
            for d in range(2, KD):
                if d % 2 == 0:
                    pe.wait_ge(w_lo, U_OUT + d // 2 + 1)
                if d >= 4:
                    pe.wait_ge(xo_added, d - 3)
                out_terms(d, order).then_inc(wo_ps, 1)

            ffn(1, 2)


def constants():
    import numpy as np

    i = np.arange(P)
    c = np.zeros((P, C_N), np.float32)
    c[:, C_ID:C_ID + P] = np.eye(P)
    c[:, C_UP:C_UP + P] = i[:, None] <= i[None, :]
    c[:, C_ONE:C_ONE + P] = 1.0
    c[:, C_NEG:C_NEG + P] = np.where(i[:, None] <= i[None, :], 0.0, -1e30)
    for l in range(LEVELS):
        s = 1 << l
        same = (i[:, None] // (2 * s)) == (i[None, :] // (2 * s))
        c[:, C_LEV + l * P:C_LEV + (l + 1) * P] = same & (i[:, None] % (2 * s) < s) & (i[None, :] % (2 * s) >= s)
    rel = np.arange(T)[None, :] - (T - P) - i[:, None]
    c[:, C_REL:C_REL + T] = np.where(rel <= 0, rel, -1e30)
    c[:, C_SEL] = i < DH
    c[:, C_SEL + 1] = i >= DH
    return c


def columns(w, start, n):
    return w[:, start:start + n].reshape(KD, P, n).transpose(1, 0, 2).reshape(P, KD * n)


def kernel(**inputs):
    import numpy as np
    import concourse.bacc as bacc
    from concourse.bass_utils import run_bass_kernel_spmd

    a = {k: np.ascontiguousarray(v) for k, v in inputs.items()}

    def ffn_units(g, u, d):
        def down(i):
            return d[256 * i:256 * (i + 1)].reshape(2, P, D).transpose(1, 0, 2).reshape(P, 2 * D)

        units = [columns(g, 0, 256), columns(u, 0, 256)]
        for i in range(1, FG):
            units += [columns(g, 256 * i, 256), columns(u, 256 * i, 256), down(i - 1)]
        return units + [down(FG - 1)]

    w_in, w_out, w_kv = a["w_in"][0], a["w_out"][0], a["w_mem_kv"][0]
    starts = [256 * i for i in range(8)] + [2056, 2312, 2824, 2568]
    units = [columns(w_kv, 0, 256), columns(w_kv, 256, 256)]
    units += ffn_units(a["ffn1_w_gate"][0], a["ffn1_w_up"][0], a["ffn1_w_down"][0])
    units += [columns(w_in, s, 256) for s in starts]
    units += [columns(w_out, 256 * i, 256) for i in range(4)]
    units += ffn_units(a["ffn2_w_gate"][0], a["ffn2_w_up"][0], a["ffn2_w_down"][0])

    def per_partition(v):
        return v.reshape(-1, P).T

    small = np.concatenate(
        [per_partition(a[n][0]) for n in ("ffn1_norm", "mix_norm", "ffn2_norm", "mem_norm")]
        + [a["gdn_conv_w"][0].reshape(4, 12, P).transpose(2, 1, 0).reshape(P, 48), a["gdn_out_norm"][0][:, None]]
        + [np.concatenate([a[n][0]] * 2)[:, None] for n in ("moba_q_norm", "moba_k_norm", "mem_q_norm", "mem_k_norm")]
        + [np.broadcast_to(a[n], (P, H)) for n in ("gdn_a_log", "gdn_dt_bias")], axis=1)
    arrays = {
        "stream": np.stack(units),
        "x_in": a["x"][0].T.reshape(KD, P, T).transpose(1, 0, 2),
        "mem_in": a["mem"][0].T.reshape(KD, P, M).transpose(1, 0, 2),
        "ab_in": w_in[:, 2048:2056].reshape(KD, P, 8).transpose(1, 0, 2),
        "small_in": small,
        "const_in": constants(),
    }
    arrays = {k: np.ascontiguousarray(v) for k, v in arrays.items()}
    nc = bacc.Bacc("TRN2", target_bir_lowering=False, num_devices=1)
    args = [nc.dram_tensor(k, v.shape, F32, kind="ExternalInput").ap() for k, v in arrays.items()]
    args.append(nc.dram_tensor("out", (P, KD, T), F32, kind="ExternalOutput").ap())
    build(nc, *args)
    got = run_bass_kernel_spmd(nc, [arrays], core_ids=[0]).results[0]["out"]
    return got.transpose(1, 0, 2).reshape(D, T).T.reshape(1, T, D)
```

```python
from contextlib import ExitStack

import concourse.bass as bass
from concourse import mybir

F32 = mybir.dt.float32
F32R = mybir.dt.float32r
ALU = mybir.AluOpType
ACT = mybir.ActivationFunctionType
AX = mybir.AxisListType

P = 128
T = 512
NC_ = T // P
D = 1024
KD = D // P
M = 256
MC = M // P
FG = 2816 // 256
H = 4
DH = 64
EPS = 1e-6
SCALE = DH ** -0.5
LEVELS = 7
SLOPES = [2.0 ** (-8.0 * (h + 1) / H) for h in range(H)]

U_FFN = [2, 2 + 3 * FG + 12 + 4]
U_IN = 2 + 3 * FG
U_OUT = U_IN + 12
UNITS = U_FFN[1] + 3 * FG
RAW = 2
RING = 3
EARLY = 3

C_ID, C_UP, C_ONE, C_NEG, C_LEV = 0, P, 2 * P, 3 * P, 4 * P
C_REL = C_LEV + LEVELS * P
C_SEL = C_REL + T
C_N = C_SEL + 2
S_G1, S_GM, S_G2, S_GMEM = 0, KD, 2 * KD, 3 * KD
S_CONV = 4 * KD
S_OG = S_CONV + 12 * 4
S_MQ, S_MK, S_CQ, S_CK = S_OG + 1, S_OG + 2, S_OG + 3, S_OG + 4
S_ALOG = S_OG + 5
S_DT = S_ALOG + H
S_N = S_DT + H


def build(nc, stream, x_in, mem_in, ab_in, small_in, const_in, out):
    with ExitStack() as ctx:
        arena_bytes = 208 * 1024
        arena = ctx.enter_context(nc.sbuf_tensor("arena", [P, (arena_bytes - 600) // 4], F32))
        base = (nc.sbuf_base - arena_bytes + 600 + 31) // 32 * 32
        cursor = [base]

        def place(name, shape, dt=F32, at=None):
            size = 4
            for n in shape[1:]:
                size *= n
            if at is None:
                at = cursor[0]
                cursor[0] += (size + 31) // 32 * 32
            return nc.alloc_sbuf_tensor_at(name, shape, dt, offset=at), at, at + (size + 31) // 32 * 32

        def sem(name):
            return ctx.enter_context(nc.semaphore(name))

        x, _, _ = place("x", [P, KD, T])
        ahi, a_hi0, _ = place("ahi", [P, KD, T], F32R)
        alo, a_lo0, _ = place("alo", [P, KD, T], F32R)
        raw, _, _ = place("raw", [P, RAW, 2048])
        whi, whi_at, _ = place("whi", [P, RING, 2048], F32R)
        wlo, wlo_at, _ = place("wlo", [P, RING, 2048], F32R)
        rbc, _, _ = place("rbc", [P, T])
        cst, _, _ = place("cst", [P, C_N])
        small, _, _ = place("small", [P, S_N])
        abr, _, _ = place("abr", [P, KD, 8])
        abhi, _, _ = place("abhi", [P, KD, 8], F32R)
        ablo, _, _ = place("ablo", [P, KD, 8], F32R)
        rtm, _, _ = place("rtm", [P, 3, NC_])
        rmem, _, _ = place("rmem", [P, MC])
        msq_, _, _ = place("stat_mean", [P, 48])
        root, _, _ = place("stat_root", [P, 48])
        newt, _, _ = place("stat_newton", [P, 48])
        inv0, _, _ = place("stat_inv", [P, 48])
        rqk, _, _ = place("rqk", [P, 8, NC_])
        ratt, _, _ = place("ratt", [P, 6, NC_, 2])
        rmk, _, _ = place("rmk", [P, 2, MC, 2])
        gain_qk, _, _ = place("gain_qk", [P, 2])
        gates, _, _ = place("gates", [P, 16, 16])
        rowmax, _, _ = place("rowmax", [P, 4])
        negmax, _, _ = place("negmax", [P, 4])
        rowsum, _, _ = place("rowsum", [P, 2, 2 * H])
        rowinv, _, _ = place("rowinv", [P, 2 * H])
        mid = cursor[0]

        qkv, _, _ = place("qkv", [P, 12, T])
        z, z_at, _ = place("z", [P, H, T])
        mq, _, _ = place("mq", [P, 2, T])
        mk, _, _ = place("mk", [P, 2, T])
        cq, _, _ = place("cq", [P, 2, T])
        mv, _, _ = place("mv", [P, NC_, M])
        ck, _, _ = place("ck", [P, 2, M])
        cv, _, _ = place("cv", [P, MC, M])
        kt, kt_at, _ = place("kt", [P, NC_, H, P])
        pt, pt_at, _ = place("pt", [P, NC_, H, P])
        xt, xt_at, _ = place("xt", [P, NC_, H, P])
        dec, dec_at, _ = place("dec", [P, H, P])
        at_, _, _ = place("at", [P, 2, H, P])
        top = cursor[0]
        assert top <= base + arena_bytes - 600, (top, base + arena_bytes)
        cin, _, nxt = place("cin", [P, 2, T + 4], at=kt_at)
        cout, _, _ = place("cout", [P, 2, T], at=nxt)
        sqk, _, _ = place("sqk", [P, 4, T], at=xt_at)
        sqa, _, _ = place("sqa", [P, 4, T], at=z_at)
        two = 2 * T * 4
        slot = (U_OUT - 1) % RING * 2048 * 4
        tmp_at = [(kt_at + two, pt_at + two, xt_at + two), (whi_at + slot, whi_at + slot + two, wlo_at + slot)]
        bm, ysb, xn = ([place(f"{n}{pair}", [P, 2, H, P], at=tmp_at[pair][i])[0] for pair in range(2)]
                       for i, n in enumerate(("bm", "ysb", "xn")))
        prob = [place("prob0", [P, T], at=wlo_at + slot + two)[0],
                place("prob1", [P, T], at=wlo_at + slot + two + T * 4)[0], rbc]
        sc, _, nxt = place("sc", [P, 2, T], at=a_hi0)
        ptr, _, _ = place("ptr", [P, 2, NC_, P], at=nxt)
        rsb, _, nxt = place("rsb", [P, H, P], at=a_lo0)
        vsb, _, nxt = place("vsb", [P, H, P], at=nxt)
        state, _, _ = place("state", [P, 2, H, P], at=nxt)
        yt, _, _ = place("yt", [P, 4, T], at=a_lo0 + 4 * T * 4)
        gbuf, _, nxt = place("gbuf", [P, 2, T], at=mid)
        hhi, _, nxt = place("hhi", [P, 4, T], F32R, at=nxt)
        hlo, _, nxt = place("hlo", [P, 4, T], F32R, at=nxt)
        sqx, _, _ = place("sqx", [P, KD, T], at=z_at)
        memx, _, nxt = place("memx", [P, KD, M], at=kt_at)
        memhi, _, nxt = place("memhi", [P, KD, M], F32R, at=nxt)
        memlo, _, nxt = place("memlo", [P, KD, M], F32R, at=nxt)
        memsq, _, nxt2 = place("memsq", [P, KD, M], at=mid)
        mksq, _, _ = place("mksq", [P, 2, M], at=nxt2)
        ahi2, _, _ = place("ahi2", [P, KD, T], F32R, at=kt_at)
        alo2, _, _ = place("alo2", [P, KD, T], F32R, at=z_at)
        sqx2, _, _ = place("sqx2", [P, KD, T], at=mid + 2 * T * 4)
        x_hi, x_lo, x_sq = (ahi, ahi, ahi2), (alo, alo, alo2), (sqx, sqx, sqx2)
        yn, _, _ = place("yn", [P, T], at=dec_at)
        abt, _, _ = place("abt", [8, T], at=dec_at)
        assert nxt <= top

        psum = [ctx.enter_context(nc.psum_tensor(f"bank{i}", [P, T], F32)) for i in range(8)]

        ident, upper = cst[:, C_ID:C_ID + P], cst[:, C_UP:C_UP + P]
        ones, negmask = cst[:, C_ONE:C_ONE + P], cst[:, C_NEG:C_NEG + P]
        headsel = cst[:, C_SEL:C_SEL + 2]

        def level(l):
            return cst[:, C_LEV + l * P:C_LEV + (l + 1) * P]

        def over_heads(ap):
            return ap.unsqueeze(1).broadcast_to([P, H, P])

        def heads(bank):
            return psum[bank][:, :].rearrange("p (h t) -> p h t", h=H)

        def col(c):
            return small[:, c:c + 1]

        (G_A, G_B, G_NEG, G_EXP, G_LN, G_G, G_EB, G_BETA, G_GC, G_GL, G_GT, G_EG, G_EGL, G_ET,
         G_RKB, G_SR) = range(16)
        G_GK = G_LN

        def gate(n, m=1):
            return gates[:, n:n + m, :]

        def gate_hc(n):
            return gates[:, n, :].rearrange("p (h c) -> p h c", h=H)

        def gcol(n, h, c):
            return gates[:, n, h * NC_ + c:h * NC_ + c + 1]

        cst_in, masks_in, small_sem, ab_sem, out_done = (
            sem(n) for n in ("cst_in", "masks_in", "small_sem", "ab_sem", "out_done"))
        mem_sems = [sem(f"mem_in{i}") for i in range(2)]
        x_sem = [sem(f"x_in{i}") for i in range(4)]
        raw_in = [sem(f"raw_in{i}") for i in range(RAW)]
        w_hi, w_lo, w_used = sem("w_hi"), sem("w_lo"), sem("w_used")
        cv_ready = sem("cv_ready")
        half_in, half_hi, half_lo = sem("half_in"), sem("half_hi"), sem("half_lo")
        dve_chain = sem("dve_chain")
        ab_hi, ab_lo = sem("ab_hi"), sem("ab_lo")
        mem_hi, mem_lo, mem_sq, mem_sum, mem_stat = (
            sem(n) for n in ("mem_hi", "mem_lo", "mem_sq", "mem_sum", "mem_stat"))
        ck_ps, cv_ps, rm_ready, rmbc_ps, rmbc_sb = (
            sem(n) for n in ("ck_ps", "cv_ps", "rm_ready", "rmbc_ps", "rmbc_sb"))
        ck_raw, ck_sq, ck_stat, rmk_ready, ckbc_ps, ck_ready = (
            sem(n) for n in ("ck_raw", "ck_sq", "ck_stat", "rmk_ready", "ckbc_ps", "ck_ready"))
        mean_ready, root_ready = sem("mean_ready"), sem("root_ready")
        a_hi, a_lo, sq_ready, stat_done = sem("a_hi"), sem("a_lo"), sem("sq_ready"), sem("stat_done")
        sq_pool = sem("sq_pool")
        rtm_ready, rbc_ps, r_ready = sem("rtm_ready"), sem("rbc_ps"), sem("r_ready")
        gate_done, gate_scaled, silu_done, up_done = (
            sem(n) for n in ("gate_done", "gate_scaled", "silu_done", "up_done"))
        silu_scaled, h_done, h_hi, h_lo = sem("silu_scaled"), sem("h_done"), sem("h_hi"), sem("h_lo")
        down_done, x_added = sem("down_done"), sem("x_added")
        p_done, p_evac, conv_done, qkv_ready = sem("p_done"), sem("p_evac"), sem("conv_done"), sem("qkv_ready")
        sqk_ready, sqk_used, z_ready = sem("sqk_ready"), sem("sqk_used"), sem("z_ready")
        sqa_ready, sqa_used = sem("sqa_ready"), sem("sqa_used")
        ab_ps, ab_sb, ab_tm = sem("ab_ps"), sem("ab_sb"), sem("ab_tm")
        g_dve, g_act, g_pe = sem("g_dve"), sem("g_act"), sem("g_pe")
        gates_ready, rqk_ready, ratt_ready = sem("gates_ready"), sem("rqk_ready"), sem("ratt_ready")
        prep_ps = [sem(f"prep_ps{i}") for i in range(6)]
        dpre, dexp, eg_ready, rb_read = sem("dpre"), sem("dexp"), sem("eg_ready"), sem("rb_read")
        kt_ready, bv_ready, qe_ready, at_ready, pt_ready = (
            sem(n) for n in ("kt_ready", "bv_ready", "qe_ready", "at_ready", "pt_ready"))
        mkbc_ps, mk_ready = sem("mkbc_ps"), sem("mk_ready")
        b_ready, bt_ps, xt_ps, xt_sb, y_ps, y_sb, xyx_ps, x_upd = (
            sem(n) for n in ("b_ready", "bt_ps", "xt_ps", "xt_sb", "y_ps", "y_sb", "xyx_ps", "x_upd"))
        sum_ready = sem("sum_ready")
        s_ps, nm_ready, exp_done, yn_ready, yt_ps, yt_sb, pt_ps, pt_sb, pv_done, yb_hi, yb_lo = (
            sem(n) for n in ("s_ps", "nm_ready", "exp_done", "yn_ready", "yt_ps", "yt_sb", "pt_ps", "pt_sb", "pv_done",
                             "yb_hi", "yb_lo"))
        ks_ps, r_sb, v_ps, v_sb, o_ps, o_sb, kv_ps, s_upd = (
            sem(n) for n in ("ks_ps", "r_sb", "v_ps", "v_sb", "o_ps", "o_sb", "kv_ps", "s_upd"))
        o_stat, ro_ready, obc_ps, y_tm, y_hi, y_lo = (
            sem(n) for n in ("o_stat", "ro_ready", "obc_ps", "y_tm", "y_hi", "y_lo"))
        wo_ps, xo_added = sem("wo_ps"), sem("xo_added")

        def wslice(parts, u, k, c0, n, width):
            s = u % RING
            return parts[:, s, k * width + c0:k * width + c0 + n]

        LAST = LEVELS - 1

        def n_x(pair, l, j):
            return 2 * (LEVELS * pair + l) + j

        def n_t(pair, l, j):
            return 2 * (LEVELS * pair + l - 1) + j

        def n_y(pair, l, j):
            return 2 * (LAST * pair + l - 1) + j

        STAT_BANKS = [(6, 7), (4, 5), (4, 5)]
        PREP_BANKS = [(3, 4, 5, 6), (3, 4, 5, 6), (7, 2, 1, 0), (7, 4, 5, 6)]
        MK_BANKS = (3, 6)
        INV_BANKS = [((3, 4), (5, 6)), ((4, 5), (6, 7))]

        def in_bank(q):
            return q % 4 if q < 16 else (q - 16) % 3

        A_PREP, A_LEVEL0, A_LEVEL, A_SCAN = 0, 4, 5, 19

        jobs = [(kind, h, c) for c in range(NC_) for kind in ("moba", "mem") for h in range(H)]
        NJ = len(jobs)
        JC = 2 * H

        block = ctx.enter_context(nc.Block())

        @block.sync
        def _(sp):
            sp.dma_start(small[:], small_in).then_inc(small_sem, 16)
            sp.dma_start(raw[:, 0, 0:1024], stream[0:1, :, 0:1024].rearrange("o p n -> (o p) n")).then_inc(half_in, 16)
            for i in range(2):
                sp.dma_start(memx[:, 4 * i:4 * i + 4, :], mem_in[:, 4 * i:4 * i + 4, :]).then_inc(mem_sems[i], 16)
            sp.dma_start(raw[:, 0, 1024:], stream[0:1, :, 1024:].rearrange("o p n -> (o p) n")).then_inc(raw_in[0], 16)
            sp.dma_start(raw[:, 1, :], stream[1:2, :, :].rearrange("o p n -> (o p) n")).then_inc(raw_in[1], 16)
            for i in range(4):
                if i == 2:
                    sp.wait_ge(w_lo, 1)
                    sp.dma_start(raw[:, 0, :], stream[2:3, :, :].rearrange("o p n -> (o p) n")).then_inc(raw_in[0], 16)
                sp.dma_start(x[:, 2 * i:2 * i + 2, :], x_in[:, 2 * i:2 * i + 2, :]).then_inc(x_sem[i], 16)
            sp.dma_start(cst[:, 0:C_LEV], const_in[:, 0:C_LEV]).then_inc(cst_in, 16)
            sp.dma_start(cst[:, C_SEL:C_N], const_in[:, C_SEL:C_N]).then_inc(cst_in, 16)
            sp.wait_ge(w_lo, 2)
            sp.dma_start(raw[:, 1, :], stream[3:4, :, :].rearrange("o p n -> (o p) n")).then_inc(raw_in[1], 16)
            sp.dma_start(abr[:], ab_in).then_inc(ab_sem, 16)
            sp.dma_start(cst[:, C_LEV:C_SEL], const_in[:, C_LEV:C_SEL]).then_inc(masks_in, 16)
            with sp.Fori(2, UNITS // RAW) as i:
                for s in range(RAW):
                    sp.wait_ge(w_lo, RAW * i + (s + 1 - RAW))
                    sp.dma_start(raw[:, s, :], stream[bass.ds(i * RAW + s, 1), :, :].rearrange("o p n -> (o p) n")
                                 ).then_inc(raw_in[s], 16)
            for d in range(KD):
                sp.wait_ge(x_added, 2 * KD * FG - KD + d + 1)
                sp.dma_start(out[:, d, :], x[:, d, :]).then_inc(out_done, 16)
            sp.wait_ge(out_done, 16 * KD)

        @block.gpsimd
        def _(pool):
            period = RAW * RING
            MIX = U_IN // period * period + period
            MIX_END = (U_OUT + 2) // period * period + period

            def split(u, count):
                pool.wait_ge(w_hi, count + 1)
                nc.gpsimd.tensor_tensor(wlo[:, u % RING, :], raw[:, u % RAW, :],
                                        whi[:, u % RING, :].bitcast(F32), ALU.subtract).then_inc(w_lo, 1)

            for d in range(4, KD):
                pool.wait_ge(x_sem[d // 2], 16)
                nc.gpsimd.tensor_tensor(sqx[:, d, :], x[:, d, :], x[:, d, :], ALU.mult).then_inc(sq_pool, 1)
            pool.wait_ge(sq_pool, 4)
            nc.gpsimd.tensor_tensor(sqx[:, 4:6, :], sqx[:, 4:6, :], sqx[:, 6:8, :], ALU.add).then_inc(sq_pool, 1)
            pool.wait_ge(w_lo, EARLY)
            for s in range(EARLY, period):
                split(s, s)
            with pool.Fori(1, MIX // period) as i:
                for s in range(period):
                    split(s, i * period + s)

            def masks(pair, l):
                for j in range(2):
                    if l == 0:
                        pool.wait_ge(at_ready, 2 * pair + j + 1)
                        if pair == 1:
                            pool.wait_ge(w_used, U_OUT)
                    elif l == 1:
                        pool.wait_ge(bt_ps, 2 * pair + j + 1)
                    else:
                        pool.wait_ge(y_ps, n_y(pair, l - 1, j) + 1)
                    nc.gpsimd.tensor_tensor(bm[pair][:, j, :, :], at_[:, j, :, :], over_heads(level(l)),
                                            ALU.mult).then_inc(b_ready, 1)

            pool.wait_ge(masks_in, 16)
            for u in range(MIX, U_IN + 12):
                split(u, u)
            for l in range(LEVELS):
                masks(0, l)
                if l in (3, 5):
                    u = U_OUT + (l - 3) // 2
                    split(u, u)
            for l in range(LEVELS):
                masks(1, l)
            for c in range(NC_):
                pool.wait_ge(yb_hi, c + 1)
                nc.gpsimd.tensor_tensor(alo[:, 4:8, c * P:(c + 1) * P], yt[:, :, c * P:(c + 1) * P],
                                        ahi[:, 4:8, c * P:(c + 1) * P].bitcast(F32), ALU.subtract).then_inc(yb_lo, 1)
            for u in range(U_OUT + 2, MIX_END):
                split(u, u)
            with pool.Fori(MIX_END // period, UNITS // period) as i:
                for s in range(period):
                    split(s, i * period + s)

        @block.scalar
        def _(act):
            A = nc.scalar

            def weight_hi(u, count=None, loads=None):
                count = u if count is None else count
                loads = u // RAW if loads is None else loads
                act.wait_ge(raw_in[u % RAW], loads * 16 + 16)
                if not (isinstance(count, int) and count < RING):
                    act.wait_ge(w_used, count + (1 - RING))
                A.activation(whi[:, u % RING, :], raw[:, u % RAW, :], ACT.Copy).then_inc(w_hi, 1)

            def sqrt(n, width):
                act.wait_ge(mean_ready, n + 1)
                A.activation(root[:, 0:width], msq_[:, 0:width], ACT.Sqrt).then_inc(root_ready, 1)

            def x_parts(stage, gain, ready, unit=None):
                for d in range(KD):
                    if d == 3 and unit is not None:
                        weight_hi(unit)
                    ready(d)
                    x_high(stage, gain, d)
                    x_square(stage, d)

            act.wait_ge(small_sem, 16)
            act.wait_ge(half_in, 16)
            A.activation(whi[:, 0, 0:1024], raw[:, 0, 0:1024], ACT.Copy).then_inc(half_hi, 1)
            for k in range(KD):
                act.wait_ge(mem_sems[k // 4], 16)
                A.activation(memhi[:, k, :], memx[:, k, :], ACT.Copy, scale=col(S_GMEM + k)).then_inc(mem_hi, 1)
            act.wait_ge(raw_in[0], 16)
            A.activation(whi[:, 0, 1024:], raw[:, 0, 1024:], ACT.Copy).then_inc(w_hi, 1)
            weight_hi(1)

            def x_high(stage, gain, d):
                A.activation(x_hi[stage][:, d, :], x[:, d, :], ACT.Copy, scale=col(gain + d)).then_inc(a_hi, 1)

            def x_square(stage, d):
                A.activation(x_sq[stage][:, d, :], x[:, d, :], ACT.Square).then_inc(sq_ready, 1)

            for d in range(KD):
                act.wait_ge(x_sem[d // 2], 16)
                x_high(0, S_G1, d)
                if d == 3:
                    weight_hi(2)
            A.activation(memsq[:, :, :], memx[:, :, :], ACT.Square).then_inc(mem_sq, 1)
            weight_hi(3)
            for d in range(4):
                x_square(0, d)
            sqrt(0, MC)
            act.wait_ge(rmbc_ps, 1)
            A.activation(rbc[:, 0:M], psum[3][:, 0:M], ACT.Copy).then_inc(rmbc_sb, 1)
            sqrt(1, NC_)
            act.wait_ge(ck_raw, 2)
            A.activation(mksq[:, :, :], ck[:, :, :], ACT.Square).then_inc(ck_sq, 1)
            act.wait_ge(ab_sem, 16)
            A.activation(abhi[:], abr[:], ACT.Copy).then_inc(ab_hi, 1)
            weight_hi(4)
            sqrt(2, 4 * MC)

            def ffn_last(f, units):
                n0, u0 = 2 * FG * f, U_FFN[f]
                i = FG - 1
                for a in range(2):
                    act.wait_ge(gate_scaled, 2 * i + (n0 + a + 1))
                    A.activation(gbuf[:, a, :], gbuf[:, a, :], ACT.Silu).then_inc(silu_done, 1)
                act.wait_ge(w_used, 3 * i + (u0 - 1))
                for a in range(2):
                    act.wait_ge(h_done, 2 * i + (n0 + a + 1))
                    A.activation(hhi[:, a, :], gbuf[:, a, :], ACT.Copy).then_inc(h_hi, 1)
                for u in units:
                    weight_hi(u)

            def ffn_pair(f, j):
                n0, u0 = 2 * FG * f, U_FFN[f]
                for b in range(2):
                    for a in range(2):
                        act.wait_ge(gate_scaled, 4 * j + (n0 + 2 * b + a + 1))
                        A.activation(gbuf[:, a, :], gbuf[:, a, :], ACT.Silu).then_inc(silu_done, 1)

                    def hi(m):
                        v = u0 + 3 * b + m
                        weight_hi(v, 6 * j + v, 3 * j + v // RAW)

                    act.wait_ge(w_used, 6 * j + (u0 + 3 * b - 1))
                    for a in range(2):
                        act.wait_ge(h_done, 4 * j + (n0 + 2 * b + a + 1))
                        A.activation(hhi[:, 2 * b + a, :], gbuf[:, a, :], ACT.Copy).then_inc(h_hi, 1)
                    hi(3)
                    hi(4)
                    hi(5)

            with act.Fori(0, FG // 2) as j:
                ffn_pair(0, j)
            ffn_last(0, (U_IN, U_IN + 1))

            x_parts(1, S_GM, lambda d: act.wait_ge(x_added, KD * (FG - 1) + d + 1))
            for n in range(9):
                weight_hi(U_IN + n + 2)
                if n == 0:
                    sqrt(3, NC_)
                if n == 8:
                    act.wait_ge(g_dve, 4)
                    A.activation(gate(G_EG, 3), gate(G_GC, 3), ACT.Exp).then_inc(g_act, 1)
                    act.wait_ge(rqk_ready, 1)
                    A.activation(gates[:, G_GK, :], rqk[:, H:2 * H, :].rearrange("p h c -> p (h c)"),
                                 ACT.Ln).then_inc(g_act, 1)
                for q in (2 * n, 2 * n + 1):
                    if q < 12:
                        act.wait_ge(conv_done, q + 1)
                        A.activation(qkv[:, q, :], cout[:, q % 2, :], ACT.Silu).then_inc(qkv_ready, 1)
                        if q < 8:
                            if q >= 4:
                                act.wait_ge(sqk_used, q - 3)
                            act.wait_ge(qkv_ready, q + 1)
                            A.activation(sqk[:, q % 4, :], qkv[:, q, :], ACT.Square).then_inc(sqk_ready, 1)
                    else:
                        t = q - 12
                        src = (mq, mk, cq)[t // 2][:, t % 2, :]
                        act.wait_ge(p_evac, q + 1)
                        if t >= 4:
                            act.wait_ge(sqa_used, t - 3)
                        A.activation(sqa[:, t % 4, :], src, ACT.Square).then_inc(sqa_ready, 1)
                if n == 5:
                    sqrt(4, 32)
                if n == 6:
                    act.wait_ge(g_dve, 1)
                    A.activation(gate(G_EXP), gate(G_NEG), ACT.Exp).then_inc(g_act, 1)
                    A.activation(gate(G_EB), gate(G_B), ACT.Exp, scale=-1.0).then_inc(g_act, 1)
                    A.activation(rowmax[:], small[:, S_ALOG:S_ALOG + H], ACT.Exp).then_inc(g_act, 1)
                    act.wait_ge(g_dve, 2)
                    A.activation(gate(G_LN), gate(G_EXP), ACT.Ln).then_inc(g_act, 1)

            def prep_decay(c):
                g = PREP_BANKS[c][0]
                act.wait_ge(dpre, c + 1)
                A.activation(dec[:], dec[:], ACT.Exp).then_inc(dexp, 1)
                A.activation(heads(g), heads(g), ACT.Exp).then_inc(eg_ready, 1)

            def prep_keys(c):
                act.wait_ge(prep_ps[4], c + 1)
                for h in range(H):
                    A.activation(kt[:, c, h, :], heads(PREP_BANKS[c][1])[:, h, :], ACT.Copy,
                                 scale=gcol(G_ET, h, c)).then_inc(kt_ready, 1)
                act.wait_ge(prep_ps[5], c + 1)
                for h in range(H):
                    A.activation(qkv[:, 8 + h, c * P:(c + 1) * P], heads(PREP_BANKS[c][2])[:, h, :],
                                 ACT.Copy, scale=gcol(G_BETA, h, c)).then_inc(bv_ready, 1)

            def level_copy(pair, l, j):
                t, y = INV_BANKS[pair][j]
                act.wait_ge(xt_ps, n_t(pair, l, j) + 1)
                A.activation(xt[:, 2 * pair + j, :, :], heads(t), ACT.Copy).then_inc(xt_sb, 1)
                if l <= LAST:
                    act.wait_ge(y_ps, n_y(pair, l, j) + 1)
                    A.activation(ysb[pair][:, j, :, :], heads(y), ACT.Copy).then_inc(y_sb, 1)

            def attention(a):
                if 2 <= a < NJ + 2:
                    kind, h, c = jobs[a - 2]
                    n = c + 1 if kind == "moba" else MC
                    act.wait_ge(pt_ps, a - 1)
                    if a >= 4:
                        act.wait_ge(pv_done, a - 3)
                    A.activation(ptr[:, a % 2, 0:n, :], heads(2)[:, 0:n, :], ACT.Copy).then_inc(pt_sb, 1)
                if a < NJ:
                    kind, h, c = jobs[a]
                    act.wait_ge(nm_ready, a + 1)
                    if a >= 3:
                        act.wait_ge(pt_ps, a - 2)
                    if a >= 2 * JC:
                        act.wait_ge(yn_ready, a // JC - 1)
                    m4 = slice(a % 4, a % 4 + 1)
                    rs = rowsum[:, c % 2, a % JC:a % JC + 1]
                    if kind == "moba":
                        w = P * (c + 1)
                        A.activation(prob[a % 3][:, 0:w], sc[:, a % 2, 0:w], ACT.Exp, bias=negmax[:, m4],
                                     scale=SLOPES[h], accum_out=rs).then_inc(exp_done, 1)
                    else:
                        A.activation(prob[a % 3][:, 0:M], psum[a % 2][:, 0:M], ACT.Exp, bias=negmax[:, m4],
                                     scale=ratt[:, 4 + h // 2, c, h % 2:h % 2 + 1],
                                     accum_out=rs).then_inc(exp_done, 1)
                if a >= JC + 3 and (a - 3) % JC == 0:
                    c = (a - 3) // JC - 1
                    act.wait_ge(yt_ps, c + 1)
                    whole = yt[:, :, c * P:(c + 1) * P]
                    A.activation(whole, heads(2), ACT.Copy).then_inc(yt_sb, 1)
                    act.wait_ge(yt_sb, c + 1)
                    A.activation(ahi[:, 4:8, c * P:(c + 1) * P], whole, ACT.Copy).then_inc(yb_hi, 1)

            act.wait_ge(gates_ready, 1)
            prep_decay(0)
            weight_hi(U_IN + 11)
            prep_keys(0)
            prep_decay(1)
            prep_keys(1)
            sqrt(5, 48)
            for l in range(1, LEVELS):
                for j in range(2):
                    level_copy(0, l, j)
                if l in (2, 4):
                    weight_hi(U_IN + 11 + l // 2)
            prep_decay(2)
            for j in range(2):
                level_copy(0, LEVELS, j)
            for t in range(H):
                act.wait_ge(p_evac, 22 + t + 1)
                A.activation(z[:, t, :], z[:, t, :], ACT.Silu).then_inc(z_ready, 1)
            prep_keys(2)
            prep_decay(3)
            for a in range(A_PREP, A_PREP + 3):
                attention(a)
            prep_keys(3)
            for a in range(A_PREP + 3, A_LEVEL0):
                attention(a)
            attention(A_LEVEL0)
            for l in range(1, LEVELS):
                for j in range(2):
                    level_copy(1, l, j)
                for i in range(2):
                    attention(A_LEVEL + 2 * (l - 1) + i)
            for j in range(2):
                level_copy(1, LEVELS, j)
            attention(A_SCAN - 2)
            attention(A_SCAN - 1)
            for a in range(A_SCAN, NJ + 4):
                if a >= A_SCAN + 4 * NC_:
                    attention(a)
                    continue
                c, s = (a - A_SCAN) // 4, (a - A_SCAN) % 4
                if s == 2:
                    act.wait_ge(v_ps, c + 1)
                    if c >= 1:
                        act.wait_ge(o_ps, c)
                    A.activation(vsb[:], heads(5), ACT.Copy).then_inc(v_sb, 1)
                attention(a)
                if s == 3:
                    act.wait_ge(o_ps, c + 1)
                    A.activation(qkv[:, 0:H, c * P:(c + 1) * P], heads(6), ACT.Copy).then_inc(o_sb, 1)
                    A.activation(qkv[:, H:2 * H, c * P:(c + 1) * P], heads(6), ACT.Square).then_inc(o_sb, 1)
            weight_hi(U_OUT + 2)
            sqrt(6, 16)
            for h in range(H):
                act.wait_ge(y_tm, h + 1)
                if h == 0:
                    act.wait_ge(exp_done, NJ)
                A.activation(ahi[:, h, :], qkv[:, 8 + h, :], ACT.Copy).then_inc(y_hi, 1)
            weight_hi(U_OUT + 3)
            weight_hi(U_OUT + 4)
            x_parts(2, S_G2, lambda d: act.wait_ge(xo_added, d + 1), U_OUT + 5)
            weight_hi(U_FFN[1] + 2)
            sqrt(7, NC_)
            with act.Fori(0, FG // 2) as j:
                ffn_pair(1, j)
            ffn_last(1, ())

        @block.vector
        def _(dve):
            V = nc.vector
            links = [0]

            def link(ins):
                links[0] += 1
                ins.then_inc(dve_chain, 1)
                dve.wait_ge(dve_chain, links[0])

            def mean(n, src, dst, scale):
                V.tensor_scalar(dst, src, scale, EPS, ALU.mult, ALU.add).then_inc(mean_ready, 1)
                dve.wait_ge(mean_ready, n + 1)

            def rsqrt(n, width, dst, done):
                m, y, t, i0 = msq_[:, 0:width], root[:, 0:width], newt[:, 0:width], inv0[:, 0:width]
                dve.wait_ge(root_ready, n + 1)
                link(V.reciprocal(i0, y))
                link(V.scalar_tensor_tensor(out=t, in0=m, scalar=-0.5, in1=i0, op0=ALU.mult, op1=ALU.mult))
                link(V.tensor_tensor(t, t, i0, ALU.mult))
                V.scalar_tensor_tensor(out=dst, in0=t, scalar=1.5, in1=i0, op0=ALU.add,
                                       op1=ALU.mult).then_inc(done, 1)

            def x_low(stage, gain, d):
                dve.wait_ge(a_hi, KD * stage + d + 1)
                V.scalar_tensor_tensor(out=x_lo[stage][:, d, :], in0=x[:, d, :], scalar=col(gain + d),
                                       in1=x_hi[stage][:, d, :].bitcast(F32), op0=ALU.mult,
                                       op1=ALU.subtract).then_inc(a_lo, 1)

            def sum_tiles(sq, done):
                link(V.tensor_tensor(sq[:, 0:4, :], sq[:, 0:4, :], sq[:, 4:8, :], ALU.add))
                link(V.tensor_tensor(sq[:, 0:2, :], sq[:, 0:2, :], sq[:, 2:4, :], ALU.add))
                V.tensor_tensor(sq[:, 0, :], sq[:, 0, :], sq[:, 1, :], ALU.add).then_inc(done, 1)

            def x_stat(stage, n):
                dve.wait_ge(sq_ready, KD * stage + 4)
                if stage == 0:
                    link(V.tensor_tensor(sqx[:, 0:2, :], sqx[:, 0:2, :], sqx[:, 2:4, :], ALU.add))
                    dve.wait_ge(sq_pool, 5)
                    link(V.tensor_tensor(sqx[:, 0:2, :], sqx[:, 0:2, :], sqx[:, 4:6, :], ALU.add))
                    V.tensor_tensor(sqx[:, 0, :], sqx[:, 0, :], sqx[:, 1, :], ALU.add).then_inc(sum_ready, 1)
                else:
                    sum_tiles(x_sq[stage], sum_ready)
                dve.wait_ge(stat_done, stage + 1)
                mean(n, psum[STAT_BANKS[stage][0]][:, 0:NC_], msq_[:, 0:NC_], 1.0 / D)
                rsqrt(n, NC_, rtm[:, stage, :], rtm_ready)
                if stage == 0:
                    dve.wait_ge(rmbc_sb, 1)
                    for j in range(2):
                        V.tensor_tensor(ck[:, j, :], psum[4 + j][:, 0:M], rbc[:, 0:M], ALU.mult).then_inc(ck_raw, 1)
                    dve.wait_ge(ab_hi, 1)
                    V.tensor_tensor(ablo[:], abr[:], abhi[:].bitcast(F32), ALU.subtract).then_inc(ab_lo, 1)
                    dve.wait_ge(ck_raw, 2)
                dve.wait_ge(rbc_ps, stage + 1)
                V.tensor_copy(rbc[:], psum[STAT_BANKS[stage][1]][:]).then_inc(r_ready, 1)
                dve.wait_ge(r_ready, stage + 1)

            dve.wait_ge(small_sem, 16)
            V.tensor_tensor(gain_qk[:, 0:1], col(S_MQ), col(S_MK), ALU.mult).then_inc(dve_chain, 1)
            V.tensor_tensor(gain_qk[:, 1:2], col(S_CQ), col(S_CK), ALU.mult).then_inc(dve_chain, 1)
            links[0] += 2
            dve.wait_ge(dve_chain, links[0])
            dve.wait_ge(half_hi, 1)
            V.tensor_tensor(wlo[:, 0, 0:1024], raw[:, 0, 0:1024], whi[:, 0, 0:1024].bitcast(F32),
                            ALU.subtract).then_inc(half_lo, 1)
            for k in range(KD):
                dve.wait_ge(mem_hi, k + 1)
                V.scalar_tensor_tensor(out=memlo[:, k, :], in0=memx[:, k, :], scalar=col(S_GMEM + k),
                                       in1=memhi[:, k, :].bitcast(F32), op0=ALU.mult,
                                       op1=ALU.subtract).then_inc(mem_lo, 1)
            dve.wait_ge(w_hi, 1)
            V.tensor_tensor(wlo[:, 0, 1024:], raw[:, 0, 1024:], whi[:, 0, 1024:].bitcast(F32),
                            ALU.subtract).then_inc(w_lo, 1)

            def weight_lo(u):
                dve.wait_ge(w_hi, u + 1)
                V.tensor_tensor(wlo[:, u % RING, :], raw[:, u % RAW, :], whi[:, u % RING, :].bitcast(F32),
                                ALU.subtract).then_inc(w_lo, 1)

            weight_lo(1)
            for d in range(KD):
                x_low(0, S_G1, d)
                if d == 3:
                    weight_lo(2)
            dve.wait_ge(mem_sq, 1)
            sum_tiles(memsq, mem_sum)
            dve.wait_ge(mem_stat, 1)
            mean(0, psum[2][:, 0:MC], msq_[:, 0:MC], 1.0 / D)
            rsqrt(0, MC, rmem[:, :], rm_ready)
            dve.wait_ge(rm_ready, 1)
            for c in range(MC):
                dve.wait_ge(cv_ps, c + 1)
                V.tensor_scalar(cv[:, c, :], psum[6 + c][:, 0:M], rmem[:, c:c + 1], None,
                                ALU.mult).then_inc(cv_ready, 1)
            def ck_finish():
                dve.wait_ge(ckbc_ps, 1)
                dve.wait_ge(ck_raw, 2)
                V.scalar_tensor_tensor(out=ck[:].rearrange("p j t -> p (j t)"), in0=psum[5][:],
                                       scalar=gain_qk[:, 1:2], in1=ck[:].rearrange("p j t -> p (j t)"),
                                       op0=ALU.mult, op1=ALU.mult).then_inc(ck_ready, 1)

            def ffn_hidden(n_of):
                for a in range(2):
                    dve.wait_ge(gate_done, n_of(a) + 1)
                    if not (isinstance(n_of(a), int) and n_of(a) < 2):
                        dve.wait_ge(h_hi, n_of(a) + (-1))
                        dve.wait_ge(h_lo, n_of(a) + (-1))
                    V.tensor_tensor(gbuf[:, a, :], psum[a][:], rbc[:], ALU.mult).then_inc(gate_scaled, 1)
                for a in range(2):
                    dve.wait_ge(silu_done, n_of(a) + 1)
                    V.tensor_tensor(gbuf[:, a, :], gbuf[:, a, :], rbc[:], ALU.mult).then_inc(silu_scaled, 1)
                for a in range(2):
                    dve.wait_ge(up_done, n_of(a) + 1)
                    dve.wait_ge(silu_scaled, n_of(a) + 1)
                    V.tensor_tensor(gbuf[:, a, :], psum[2 + a][:], gbuf[:, a, :], ALU.mult).then_inc(h_done, 1)

            def ffn_low(n_of, b):
                for a in range(2):
                    dve.wait_ge(h_hi, n_of(a) + 1)
                    V.tensor_tensor(hlo[:, 2 * b + a, :], gbuf[:, a, :], hhi[:, 2 * b + a, :].bitcast(F32),
                                    ALU.subtract).then_inc(h_lo, 1)

            def ffn_add(before, d):
                dve.wait_ge(down_done, before + (d + 1))
                V.scalar_tensor_tensor(out=x[:, d, :], in0=psum[4 + d % 4][:], scalar=0.5, in1=x[:, d, :],
                                       op0=ALU.mult, op1=ALU.add).then_inc(x_added, 1)

            def ffn(f):
                n0, d0 = 2 * FG * f, KD * FG * f
                ffn_hidden(lambda a: n0 + a)
                ffn_low(lambda a: n0 + a, 0)
                if f == 0:
                    ck_finish()
                with dve.Fori(0, FG // 2) as j:
                    for b in range(2):
                        n_of = lambda a, b=b: 4 * j + (n0 + 2 * (b + 1) + a)
                        ffn_hidden(n_of)
                        ffn_low(n_of, 1 - b)
                        dve.wait_ge(gate_scaled, 4 * j + (n0 + 2 * b + 4))
                        for d in range(KD):
                            ffn_add(2 * KD * j + (d0 + KD * b), d)
                dve.wait_ge(x_added, d0 + KD * (FG - 1))

            x_stat(0, 1)
            dve.wait_ge(ck_stat, 1)
            mean(2, psum[4][:, 0:4 * MC], msq_[:, 0:4 * MC], 1.0 / DH)
            rsqrt(2, 4 * MC, rmk[:].rearrange("p j c e -> p (j c e)"), rmk_ready)
            ffn(0)
            for d in range(KD):
                ffn_add(KD * (FG - 1), d)
                if d >= 1:
                    x_low(1, S_GM, d - 1)
            x_low(1, S_GM, KD - 1)

            V.memset(cin[:, :, 0:3], 0.0).then_inc(dve_chain, 1)
            links[0] += 1
            x_stat(1, 3)
            dve.wait_ge(dve_chain, links[0])

            def evacuate(q, dst):
                dve.wait_ge(p_done, q + 1)
                V.tensor_tensor(dst, psum[in_bank(q)][:], rbc[:], ALU.mult).then_inc(p_evac, 1)

            def conv(q):
                o, i = cout[:, q % 2, :], cin[:, q % 2, :]
                dve.wait_ge(p_evac, q + 1)
                if q >= 2:
                    dve.wait_ge(qkv_ready, q - 1)
                w = S_CONV + 4 * q
                link(V.tensor_scalar(o, i[:, 0:T], col(w), None, ALU.mult))
                for j in (1, 2):
                    link(V.scalar_tensor_tensor(out=o, in0=i[:, j:j + T], scalar=col(w + j), in1=o,
                                                op0=ALU.mult, op1=ALU.add))
                V.scalar_tensor_tensor(out=o, in0=i[:, 3:3 + T], scalar=col(w + 3), in1=o,
                                       op0=ALU.mult, op1=ALU.add).then_inc(conv_done, 1)

            for q in range(12):
                if q >= 2:
                    dve.wait_ge(conv_done, q - 1)
                evacuate(q, cin[:, q % 2, 3:3 + T])
                conv(q)
            dve.wait_ge(ab_ps, 1)
            V.tensor_copy(abt[:, :], psum[6][0:8, :]).then_inc(ab_sb, 1)
            dve.wait_ge(sqk_used, 8)
            mean(4, psum[7][:, 0:32], msq_[:, 0:32], 1.0)
            dve.wait_ge(conv_done, 12)
            for q in range(12, 14):
                evacuate(q, mq[:, q % 2, :])
            dve.wait_ge(ab_tm, 1)
            abv = psum[6][:, 0:32].rearrange("p (c n) -> p c n", c=NC_)
            for c in range(NC_):
                V.scalar_tensor_tensor(out=gate_hc(G_A)[:, :, c], in0=abv[:, c, 0:H], scalar=rtm[:, 1, c:c + 1],
                                       in1=small[:, S_DT:S_DT + H], op0=ALU.mult, op1=ALU.add).then_inc(dve_chain, 1)
                V.tensor_scalar(gate_hc(G_B)[:, :, c], abv[:, c, H:2 * H], rtm[:, 1, c:c + 1], None,
                                ALU.mult).then_inc(dve_chain, 1)
                links[0] += 2
            dve.wait_ge(dve_chain, links[0])
            V.scalar_tensor_tensor(out=gate(G_NEG), in0=gate(G_A), scalar=-1.0, in1=gate(G_A), op0=ALU.mult,
                                   op1=ALU.min).then_inc(g_dve, 1)
            rsqrt(4, 32, rqk[:].rearrange("p t c -> p (t c)"), rqk_ready)
            dve.wait_ge(g_act, 1)
            V.tensor_scalar(gate(G_EXP), gate(G_EXP), 1.0, None, ALU.add).then_inc(g_dve, 1)
            dve.wait_ge(g_act, 2)
            link(V.tensor_scalar(gate(G_EB), gate(G_EB), 1.0, None, ALU.add))
            link(V.reciprocal(gate(G_BETA), gate(G_EB)))
            dve.wait_ge(g_act, 4)
            link(V.scalar_tensor_tensor(out=gate(G_LN), in0=gate(G_A), scalar=0.0, in1=gate(G_LN), op0=ALU.max,
                                        op1=ALU.add))
            V.scalar_tensor_tensor(out=gate_hc(G_G), in0=gate_hc(G_LN), scalar=-1.0,
                                   in1=rowmax[:].unsqueeze(2).broadcast_to([P, H, NC_]), op0=ALU.mult,
                                   op1=ALU.mult).then_inc(g_dve, 1)
            for q in range(14, 16):
                evacuate(q, mk[:, q % 2, :])
            dve.wait_ge(g_pe, 1)
            link(V.tensor_copy(gates[:, G_GC:G_GC + 2, :], psum[6][:, 64:96].rearrange("p (n m) -> p n m", n=2)))
            V.tensor_tensor(gate(G_GT), gate(G_GL), gate(G_GC), ALU.subtract).then_inc(g_dve, 1)
            for q in range(16, 18):
                evacuate(q, cq[:, q % 2, :])
            dve.wait_ge(g_act, 6)
            dve.wait_ge(rqk_ready, 1)
            link(V.tensor_tensor(gates[:, G_GK, :], gates[:, G_GC, :], gates[:, G_GK, :], ALU.subtract))
            rq = rqk[:, 0:H, :].rearrange("p h c -> p (h c)")
            rk = rqk[:, H:2 * H, :].rearrange("p h c -> p (h c)")
            link(V.tensor_tensor(gates[:, G_RKB, :], rk, gates[:, G_BETA, :], ALU.mult))
            link(V.scalar_tensor_tensor(out=gate(G_SR), in0=gate(G_RKB), scalar=-1.0, in1=gate(G_EG), op0=ALU.mult,
                                        op1=ALU.mult))
            link(V.tensor_tensor(gates[:, G_ET, :], rk, gates[:, G_ET, :], ALU.mult))
            V.tensor_scalar(rq, rq, float(P) ** -0.5, None, ALU.mult).then_inc(gates_ready, 1)

            def mv_evacuate(c):
                dve.wait_ge(p_done, 18 + c + 1)
                V.tensor_scalar(mv[:, c, :], psum[in_bank(18 + c)][:, 0:M], rtm[:, 1, c:c + 1], None,
                                ALU.mult).then_inc(p_evac, 1)

            def prep_decay(c):
                dve.wait_ge(prep_ps[0], c + 1)
                if c >= 1:
                    dve.wait_ge(at_ready, c)
                    dve.wait_ge(pt_ready, c)
                for h in range(H):
                    i = V.scalar_tensor_tensor(out=dec[:, h, :], in0=heads(PREP_BANKS[c][0])[:, h, :],
                                               scalar=gcol(G_GK, h, c), in1=negmask, op0=ALU.subtract, op1=ALU.add)
                i.then_inc(dpre, 1)

            def prep(c):
                gb, rb, kb, qb = PREP_BANKS[c]
                dve.wait_ge(prep_ps[1], c + 1)
                dve.wait_ge(dexp, c + 1)
                if c >= 2:
                    dve.wait_ge(b_ready, n_x(1, 0, 0))
                V.tensor_tensor(at_[:, c % 2, :, :], heads(rb), dec[:], ALU.mult).then_inc(rb_read, 1)
                dve.wait_ge(rb_read, c + 1)
                dve.wait_ge(prep_ps[2], c + 1)
                V.tensor_tensor(at_[:, c % 2, :, :], heads(kb), at_[:, c % 2, :, :], ALU.mult).then_inc(at_ready, 1)
                dve.wait_ge(prep_ps[3], c + 1)
                V.tensor_tensor(pt[:, c, :, :], heads(qb), dec[:], ALU.mult).then_inc(pt_ready, 1)
                dve.wait_ge(eg_ready, c + 1)
                V.tensor_tensor(qkv[:, 0:H, c * P:(c + 1) * P], qkv[:, 0:H, c * P:(c + 1) * P], heads(gb),
                                ALU.mult).then_inc(qe_ready, 1)

            def level_zero(pair):
                for j in range(2):
                    dve.wait_ge(bt_ps, 2 * pair + j + 1)
                    V.tensor_tensor(xn[pair][:, j, :, :], over_heads(ident), heads(INV_BANKS[pair][j][1]),
                                    ALU.subtract).then_inc(x_upd, 1)

            def level_update(pair, l):
                for j in range(2):
                    x_j = xn[pair][:, j, :, :]
                    dve.wait_ge(xyx_ps, n_y(pair, l, j) + 1)
                    dve.wait_ge(x_upd, n_x(pair, l - 1, j) + 1)
                    V.tensor_tensor(x_j, x_j, heads(INV_BANKS[pair][j][1]), ALU.subtract).then_inc(x_upd, 1)

            def attention(a):
                if a < NJ:
                    kind, h, c = jobs[a]
                    m4 = slice(a % 4, a % 4 + 1)
                    dve.wait_ge(s_ps, a + 1)
                    if a >= 2:
                        dve.wait_ge(exp_done, a - 1)
                    if kind == "moba":
                        w = P * (c + 1)
                        r = ratt[:, h // 2, c, h % 2:h % 2 + 1]
                        rel = cst[:, C_REL + T - w:C_REL + T]
                        link(V.scalar_tensor_tensor(out=sc[:, a % 2, 0:w], in0=psum[a % 2][:, 0:w], scalar=r,
                                                    in1=rel, op0=ALU.mult, op1=ALU.add))
                        link(V.tensor_reduce(rowmax[:, m4], sc[:, a % 2, 0:w], AX.X, ALU.max))
                        V.tensor_scalar(negmax[:, m4], rowmax[:, m4], -SLOPES[h], None, ALU.mult).then_inc(nm_ready, 1)
                    else:
                        r = ratt[:, 4 + h // 2, c, h % 2:h % 2 + 1]
                        link(V.tensor_reduce(rowmax[:, m4], psum[a % 2][:, 0:M], AX.X, ALU.max))
                        V.tensor_scalar(negmax[:, m4], rowmax[:, m4], r, -1.0, ALU.mult,
                                        ALU.mult).then_inc(nm_ready, 1)
                if a >= JC + 2 and (a - 2) % JC == 0:
                    c = (a - 2) // JC - 1
                    dve.wait_ge(exp_done, JC * (c + 1))
                    link(V.reciprocal(rowinv[:], rowsum[:, c % 2, :]))
                    dve.wait_ge(pv_done, JC * (c + 1))
                    if c >= 1:
                        dve.wait_ge(yt_ps, c)
                    V.tensor_tensor(yn[:].rearrange("p (h e) -> p h e", h=2 * H),
                                    psum[3][:].rearrange("p (h e) -> p h e", h=2 * H),
                                    rowinv[:].unsqueeze(2).broadcast_to([P, 2 * H, DH]),
                                    ALU.mult).then_inc(yn_ready, 1)

            for c in range(2):
                prep_decay(c)
                prep(c)
                mv_evacuate(2 * c)
                mv_evacuate(2 * c + 1)
            dve.wait_ge(sqa_used, 6)
            mean(5, psum[7][:, 0:48], msq_[:, 0:48], 1.0 / DH)
            level_zero(0)
            rsqrt(5, 48, ratt[:].rearrange("p t c e -> p (t c e)"), ratt_ready)
            dve.wait_ge(ratt_ready, 1)
            for h in range(H):
                for t0, s in ((0, SCALE / SLOPES[h]), (4, SCALE)):
                    r = ratt[:, t0 + h // 2, :, h % 2]
                    link(V.tensor_scalar(r, r, s, None, ALU.mult))
            for l in range(1, LEVELS):
                if l <= 4:
                    evacuate(21 + l, z[:, l - 1, :])
                level_update(0, l)
                if l == LAST - 1:
                    prep_decay(2)
            prep(2)
            prep_decay(3)
            for t in range(2):
                dve.wait_ge(mkbc_ps, t + 1)
                V.scalar_tensor_tensor(out=mk[:, t, :], in0=psum[MK_BANKS[t]][:], scalar=gain_qk[:, 0:1],
                                       in1=mk[:, t, :], op0=ALU.mult, op1=ALU.mult).then_inc(mk_ready, 1)
            attention(A_PREP)
            attention(A_PREP + 1)
            prep(3)
            for a in range(A_PREP + 2, A_LEVEL0):
                attention(a)
            level_zero(1)
            attention(A_LEVEL0)
            for l in range(1, LEVELS):
                attention(A_LEVEL + 2 * (l - 1))
                level_update(1, l)
                attention(A_LEVEL + 2 * (l - 1) + 1)
            attention(A_SCAN - 2)
            attention(A_SCAN - 1)
            for a in range(A_SCAN, NJ + 4):
                if a >= A_SCAN + 4 * NC_:
                    attention(a)
                    continue
                c, s = (a - A_SCAN) // 4, (a - A_SCAN) % 4
                if s == 1 and c >= 1:
                    dve.wait_ge(ks_ps, c)
                    if c >= 2:
                        dve.wait_ge(v_ps, c)
                    for h in range(H):
                        V.scalar_tensor_tensor(out=rsb[:, h, :], in0=heads(4)[:, h, :], scalar=gcol(G_SR, h, c),
                                               in1=qkv[:, 8 + h, c * P:(c + 1) * P], op0=ALU.mult,
                                               op1=ALU.add).then_inc(r_sb, 1)
                if s == 3 and c < NC_ - 1:
                    dve.wait_ge(kv_ps, c + 1)
                    if c == 0:
                        V.tensor_copy(state[:, 1, :, :], heads(7)).then_inc(s_upd, 4)
                    else:
                        dve.wait_ge(s_upd, 4 * c)
                        for h in range(H):
                            V.scalar_tensor_tensor(out=state[:, (c + 1) % 2, h, :], in0=state[:, c % 2, h, :],
                                                   scalar=gcol(G_EGL, h, c), in1=heads(7)[:, h, :],
                                                   op0=ALU.mult, op1=ALU.add).then_inc(s_upd, 1)
                attention(a)

            dve.wait_ge(o_stat, 1)
            link(V.tensor_tensor(inv0[:, 0:16], rq, rq, ALU.mult))
            link(V.scalar_tensor_tensor(out=newt[:, 0:16], in0=psum[0][:, 0:16], scalar=1.0 / P, in1=inv0[:, 0:16],
                                        op0=ALU.mult, op1=ALU.mult))
            mean(6, newt[:, 0:16], msq_[:, 0:16], 1.0)
            rsqrt(6, 16, gates[:, G_A, :], dve_chain)
            links[0] += 1
            dve.wait_ge(dve_chain, links[0])
            V.tensor_tensor(gates[:, G_B, :], gates[:, G_A, :], rq, ALU.mult).then_inc(ro_ready, 1)
            dve.wait_ge(z_ready, H)
            for h in range(H):
                yv = qkv[:, 8 + h, :]
                dve.wait_ge(obc_ps, h + 1)
                link(V.scalar_tensor_tensor(out=yv, in0=psum[h][:], scalar=col(S_OG), in1=qkv[:, h, :],
                                            op0=ALU.mult, op1=ALU.mult))
                V.tensor_tensor(yv, yv, z[:, h, :], ALU.mult).then_inc(y_tm, 1)
                if h >= 1:
                    dve.wait_ge(y_hi, h)
                    V.tensor_tensor(alo[:, h - 1, :], qkv[:, 7 + h, :], ahi[:, h - 1, :].bitcast(F32),
                                    ALU.subtract).then_inc(y_lo, 1)
            dve.wait_ge(y_hi, H)
            V.tensor_tensor(alo[:, H - 1, :], qkv[:, 11, :], ahi[:, H - 1, :].bitcast(F32),
                            ALU.subtract).then_inc(y_lo, 1)
            for d in range(KD):
                dve.wait_ge(wo_ps, d + 1)
                V.tensor_tensor(x[:, d, :], x[:, d, :], psum[4 + d % 4][:], ALU.add).then_inc(xo_added, 1)
                if d >= 1:
                    x_low(2, S_G2, d - 1)
            x_low(2, S_G2, KD - 1)
            x_stat(2, 7)
            ffn(1)
            for d in range(KD):
                ffn_add(KD * (2 * FG - 1), d)

        @block.tensor
        def _(pe):
            E = nc.tensor

            def split_product(dst, w, act_, n, last, flip=False, used=0):
                terms = ((w[0], act_[0]), (w[0], act_[1]), (w[1], act_[0]))
                if flip:
                    terms = tuple((b, a) for a, b in terms)
                for i, (a, b) in enumerate(terms):
                    ins = E.matmul(dst, a, b, start=(n == 0 and i == 0), stop=(n == last and i == 2))
                    if used and i == 0:
                        ins.then_inc(w_used, int(used))
                return ins

            def wparts(u, k, c0, n, width):
                return wslice(whi, u, k, c0, n, width), wslice(wlo, u, k, c0, n, width)

            def x_stats(stage):
                pe.wait_ge(sum_ready, stage + 1)
                for c in range(NC_):
                    i = E.matmul(psum[STAT_BANKS[stage][0]][:, c:c + 1], x_sq[stage][:, 0, c * P:(c + 1) * P], ones[:, 0:1],
                                 start=True, stop=True)
                    if c == 0:
                        i.then_inc(w_used, 1)
                i.then_inc(stat_done, 1)

            def spread(bank, c0, column):
                return E.matmul(psum[bank][:, c0:c0 + P], column, ident, start=True, stop=True)

            def spread_pair(bank, c0, two, used=False):
                for e in range(2):
                    i = E.matmul(psum[bank][e * DH:(e + 1) * DH, c0:c0 + P], two[:, e:e + 1].broadcast_to([P, DH]),
                                 ident, start=True, stop=True)
                    if used and e == 0:
                        i.then_inc(w_used, 1)
                return i

            def x_spread(stage):
                pe.wait_ge(rtm_ready, stage + 1)
                for c in range(NC_):
                    i = spread(STAT_BANKS[stage][1], c * P, rtm[:, stage, c:c + 1].broadcast_to([P, P]))
                i.then_inc(rbc_ps, 1)

            pe.wait_ge(half_lo, 1)
            for k in range(KD):
                pe.wait_ge(mem_lo, k + 1)
                if k == KD // 2:
                    pe.wait_ge(w_lo, 1)
                for j in range(2):
                    i = split_product(psum[4 + j][:, 0:M], wparts(0, k, j * P, P, 256),
                                      (memhi[:, k, :], memlo[:, k, :]), k, KD - 1)
                    if k == KD - 1:
                        i.then_inc(ck_ps, 1)
            pe.wait_ge(w_lo, 2)
            for c in range(MC):
                for k in range(KD):
                    i = split_product(psum[6 + c][:, 0:M], wparts(1, k, 0, M, 256),
                                      (memhi[:, k, c * P:(c + 1) * P], memlo[:, k, c * P:(c + 1) * P]),
                                      k, KD - 1, flip=True, used=c == 0 and k == 0)
                i.then_inc(cv_ps, 1)

            def mem_stats():
                pe.wait_ge(cst_in, 32)
                pe.wait_ge(mem_sum, 1)
                for c in range(MC):
                    i = E.matmul(psum[2][:, c:c + 1], memsq[:, 0, c * P:(c + 1) * P], ones[:, 0:1],
                                 start=True, stop=True)
                i.then_inc(mem_stat, 1)

            def mem_spread():
                pe.wait_ge(rm_ready, 1)
                for c in range(MC):
                    i = spread(3, c * P, rmem[:, c:c + 1].broadcast_to([P, P]))
                i.then_inc(rmbc_ps, 1)

            def ck_stats():
                pe.wait_ge(ck_sq, 1)
                for j in range(2):
                    for c in range(MC):
                        n = 2 * (j * MC + c)
                        i = E.matmul(psum[4][:, n:n + 2], mksq[:, j, c * P:(c + 1) * P], headsel,
                                     start=True, stop=True)
                i.then_inc(ck_stat, 1)

            def ck_spread():
                pe.wait_ge(rmk_ready, 1)
                for j in range(2):
                    for c in range(MC):
                        i = spread_pair(5, j * M + c * P, rmk[:, j, c, :])
                i.then_inc(ckbc_ps, 1)

            def up_tile(u, a, bank, done, free=None, used=False, stage=0):
                if free is not None:
                    pe.wait_ge(*free)
                for k in range(KD):
                    i = split_product(psum[bank][:], wparts(u, k, a * P, P, 256),
                                      (x_hi[stage][:, k, :], x_lo[stage][:, k, :]), k, KD - 1, used=used and k == 0)
                return i.then_inc(done, 1)

            def down(u, b, free):
                for d in range(KD):
                    if d >= 4:
                        pe.wait_ge(x_added, free + (d - 3))
                    for k in range(2):
                        i = split_product(psum[4 + d % 4][:], wparts(u, k, d * P, P, D),
                                          (hhi[:, 2 * b + k, :], hlo[:, 2 * b + k, :]), k, 1,
                                          used=d == 0 and k == 0)
                    i.then_inc(down_done, 1)

            def ffn(f, stage):
                n0, u0, d0 = 2 * FG * f, U_FFN[f], KD * FG * f
                pe.wait_ge(w_lo, u0 + 1)
                for k in range(KD):
                    pe.wait_ge(a_lo, KD * stage + k + 1)
                    i = split_product(psum[0][:], wparts(u0, k, 0, P, 256),
                                      (x_hi[stage][:, k, :], x_lo[stage][:, k, :]), k, KD - 1,
                                      used=k == 0)
                i.then_inc(gate_done, 1)
                if f == 0:
                    mem_stats()
                up_tile(u0, 1, 1, gate_done, stage=stage)
                if f == 0:
                    mem_spread()
                    pe.wait_ge(mean_ready, 1)
                    pe.wait_ge(cv_ready, MC)
                pe.wait_ge(w_lo, u0 + 2)
                x_stats(stage)
                up_tile(u0 + 1, 0, 2, up_done, stage=stage)
                x_spread(stage)
                if f == 0:
                    pe.wait_ge(rmbc_sb, 1)
                    ck_stats()
                up_tile(u0 + 1, 1, 3, up_done, stage=stage)
                if f == 0:
                    ck_spread()
                with pe.Fori(0, FG // 2) as j:
                    for b in range(2):
                        v = u0 + 2 + 3 * b
                        pe.wait_ge(w_lo, 6 * j + (v + 1))
                        for a in range(2):
                            up_tile(v, a, a, gate_done, (gate_scaled, 4 * j + (n0 + 2 * b + a + 1)), a == 0, stage)
                        pe.wait_ge(w_lo, 6 * j + (v + 2))
                        for a in range(2):
                            up_tile(v + 1, a, 2 + a, up_done, (h_done, 4 * j + (n0 + 2 * b + a + 1)), a == 0,
                                    stage)
                        pe.wait_ge(w_lo, 6 * j + (v + 3))
                        pe.wait_ge(h_lo, 4 * j + (n0 + 2 * b + 2))
                        pe.wait_ge(gate_scaled, 4 * j + (n0 + 2 * b + 4))
                        down(v + 2, b, 2 * KD * j + (d0 + KD * b))
                pe.wait_ge(w_lo, u0 + 3 * FG)
                pe.wait_ge(h_lo, n0 + 2 * FG)
                pe.wait_ge(x_added, d0 + KD * (FG - 1))
                down(u0 + 3 * FG - 1, 0, d0 + KD * (FG - 1))

            ffn(0, 0)

            def in_tile(q, n, a):
                if q >= 4:
                    pe.wait_ge(p_evac, q - 3 if q < 19 else q - 2)
                up_tile(U_IN + n, a, in_bank(q), p_done, used=n >= 2 and a == 0)

            def mv_tile(c):
                q = 18 + c
                pe.wait_ge(p_evac, q - 3 if q < 19 else q - 2)
                for k in range(KD):
                    i = split_product(psum[in_bank(q)][:, 0:M], wparts(U_IN + 9, k, 0, M, 256),
                                      (ahi[:, k, c * P:(c + 1) * P], alo[:, k, c * P:(c + 1) * P]),
                                      k, KD - 1, flip=True, used=c == 0 and k == 0)
                i.then_inc(p_done, 1)

            def att_stats(t):
                pe.wait_ge(sqa_ready, t + 1)
                if t == 0:
                    pe.wait_ge(mean_ready, 5)
                for c in range(NC_):
                    m = 2 * (t * NC_ + c)
                    i = E.matmul(psum[7][:, m:m + 2], sqa[:, t % 4, c * P:(c + 1) * P], headsel,
                                 start=True, stop=True)
                i.then_inc(sqa_used, 1)

            for n in range(9):
                pe.wait_ge(w_lo, U_IN + n + 1)
                if n == 0:
                    for k in range(KD):
                        pe.wait_ge(a_lo, KD + k + 1)
                        i = split_product(psum[0][:], wparts(U_IN, k, 0, P, 256), (ahi[:, k, :], alo[:, k, :]),
                                          k, KD - 1, used=k == 0)
                    i.then_inc(p_done, 1)
                    in_tile(1, 0, 1)
                    x_stats(1)
                    continue
                in_tile(2 * n, n, 0)
                if n == 1:
                    x_spread(1)
                in_tile(2 * n + 1, n, 1)
                if 2 <= n < 6:
                    for t in (2 * n - 4, 2 * n - 3):
                        pe.wait_ge(sqk_ready, t + 1)
                        for c in range(NC_):
                            m = t * NC_ + c
                            i = E.matmul(psum[7][:, m:m + 1], sqk[:, t % 4, c * P:(c + 1) * P], ones[:, 0:1],
                                         start=True, stop=True)
                        i.then_inc(sqk_used, 1)
                if n == 5:
                    pe.wait_ge(ab_lo, 1)
                    for k in range(KD):
                        i = split_product(psum[6][0:8, :], (abhi[:, k, :], ablo[:, k, :]),
                                          (ahi[:, k, :], alo[:, k, :]), k, KD - 1)
                    i.then_inc(ab_ps, 1)
                if n == 6:
                    pe.wait_ge(ab_sb, 1)
                    for c in range(NC_):
                        i = E.matmul(psum[6][:, 8 * c:8 * c + 8], abt[:, c * P:(c + 1) * P], ident[0:8, 0:8],
                                     is_transpose=True, start=True, stop=True)
                    i.then_inc(ab_tm, 1)
                if n == 7:
                    pe.wait_ge(g_dve, 3)
                    E.matmul(psum[6][:, 64:80], upper, gates[:, G_G, :], start=True, stop=True)
                    E.matmul(psum[6][:, 80:96], ones, gates[:, G_G, :], start=True, stop=True).then_inc(g_pe, 1)
                if n >= 7:
                    att_stats(2 * n - 14)
                    att_stats(2 * n - 13)

            def prep_decay(c):
                if c == 0:
                    pe.wait_ge(gates_ready, 1)
                    pe.wait_ge(p_evac, 16)
                    pe.wait_ge(qkv_ready, 12)
                elif c == 2:
                    pe.wait_ge(mean_ready, 6)
                else:
                    pe.wait_ge(qe_ready, c)
                for h in range(H):
                    i = E.matmul(heads(PREP_BANKS[c][0])[:, h, :], gcol(G_G, h, c).broadcast_to([P, P]), upper,
                                 start=True, stop=True)
                i.then_inc(prep_ps[0], 1)

            def prep(c):
                cs = slice(c * P, (c + 1) * P)
                gb, rb, kb, qb = PREP_BANKS[c]
                if c >= 1:
                    pe.wait_ge(kt_ready, 4 * c)
                    pe.wait_ge(bv_ready, 4 * c)
                    pe.wait_ge(pt_ready, c)
                for h in range(H):
                    i = E.matmul(heads(rb)[:, h, :], gcol(G_RKB, h, c).broadcast_to([P, P]), ident,
                                 start=True, stop=True)
                i.then_inc(prep_ps[1], 1)
                for h in range(H):
                    i = E.matmul(heads(kb)[:, h, :], qkv[:, 4 + h, cs], qkv[:, 4 + h, cs], start=True, stop=True)
                i.then_inc(prep_ps[2], 1)
                for h in range(H):
                    i = E.matmul(heads(qb)[:, h, :], qkv[:, 4 + h, cs], qkv[:, h, cs], start=True, stop=True)
                i.then_inc(prep_ps[3], 1)

            def prep_turn(c):
                cs = slice(c * P, (c + 1) * P)
                _, rb, kb, _ = PREP_BANKS[c]
                pe.wait_ge(rb_read, c + 1)
                for h in range(H):
                    i = E.transpose(heads(rb)[:, h, :], qkv[:, 4 + h, cs], ident)
                i.then_inc(prep_ps[4], 1)
                pe.wait_ge(at_ready, c + 1)
                for h in range(H):
                    i = E.transpose(heads(kb)[:, h, :], qkv[:, 8 + h, cs], ident)
                i.then_inc(prep_ps[5], 1)

            def level_zero(pair):
                c = 2 * pair + 2
                pe.wait_ge(kt_ready, 4 * c)
                pe.wait_ge(bv_ready, 4 * c)
                pe.wait_ge(pt_ready, c)
                pe.wait_ge(qe_ready, c)
                for j in range(2):
                    pe.wait_ge(b_ready, n_x(pair, 0, j) + 1)
                    for h in range(H):
                        i = E.transpose(heads(INV_BANKS[pair][j][1])[:, h, :], bm[pair][:, j, h, :], ident)
                    i.then_inc(bt_ps, 1)

            def level_turn(pair, l, j):
                pe.wait_ge(x_upd, n_x(pair, l - 1, j) + 1)
                if l >= 2:
                    pe.wait_ge(xt_sb, n_t(pair, l - 1, j) + 1)
                for h in range(H):
                    i = E.transpose(heads(INV_BANKS[pair][j][0])[:, h, :], xn[pair][:, j, h, :], ident)
                i.then_inc(xt_ps, 1)

            def level_first(pair, l):
                for j in range(2):
                    level_turn(pair, l, j)
                    pe.wait_ge(b_ready, n_x(pair, l, j) + 1)
                    for h in range(H):
                        i = E.matmul(heads(INV_BANKS[pair][j][1])[:, h, :], bm[pair][:, j, h, :],
                                     xn[pair][:, j, h, :], start=True, stop=True)
                    i.then_inc(y_ps, 1)

            def level_second(pair, l):
                for j in range(2):
                    pe.wait_ge(xt_sb, n_t(pair, l, j) + 1)
                    pe.wait_ge(y_sb, n_y(pair, l, j) + 1)
                    for h in range(H):
                        i = E.matmul(heads(INV_BANKS[pair][j][1])[:, h, :], xt[:, 2 * pair + j, h, :],
                                     ysb[pair][:, j, h, :], start=True, stop=True)
                    i.then_inc(xyx_ps, 1)

            def attention(a):
                if a < NJ:
                    kind, h, c = jobs[a]
                    if a >= 2:
                        if jobs[a - 2][0] == "moba":
                            pe.wait_ge(nm_ready, a - 1)
                        else:
                            pe.wait_ge(exp_done, a - 1)
                    r = slice(DH * (h % 2), DH * (h % 2) + DH)
                    cs = slice(c * P, (c + 1) * P)
                    if kind == "moba":
                        w = P * (c + 1)
                        E.matmul(psum[a % 2][:, 0:w], mq[r, h // 2, cs], mk[r, h // 2, 0:w], start=True,
                                 stop=True).then_inc(s_ps, 1)
                    else:
                        E.matmul(psum[a % 2][:, 0:M], cq[r, h // 2, cs], ck[r, h // 2, :], start=True,
                                 stop=True).then_inc(s_ps, 1)
                if 2 <= a < NJ + 2:
                    kind, h, c = jobs[a - 2]
                    n = c + 1 if kind == "moba" else MC
                    pe.wait_ge(exp_done, a - 1)
                    if a >= 3:
                        pe.wait_ge(pt_sb, a - 2)
                    if a >= JC + 4 and (a - 4) % JC == 0:
                        pe.wait_ge(yt_sb, (a - 4) // JC)
                    for b in range(n):
                        i = E.transpose(heads(2)[:, b, :], prob[(a - 2) % 3][:, b * P:(b + 1) * P], ident)
                    i.then_inc(pt_ps, 1)
                if 3 <= a < NJ + 3:
                    kind, h, c = jobs[a - 3]
                    n = c + 1 if kind == "moba" else MC
                    val = mv if kind == "moba" else cv
                    t = h + (0 if kind == "moba" else H)
                    pe.wait_ge(pt_sb, a - 2)
                    if (a - 3) % JC == 0 and c >= 1:
                        pe.wait_ge(yn_ready, c)
                    for b in range(n):
                        i = E.matmul(psum[3][:, t * DH:(t + 1) * DH], ptr[:, (a - 1) % 2, b, :],
                                     val[:, b, h * DH:(h + 1) * DH], start=(b == 0), stop=(b == n - 1))
                    i.then_inc(pv_done, 1)
                if a >= JC + 3 and (a - 3) % JC == 0:
                    c = (a - 3) // JC - 1
                    pe.wait_ge(yn_ready, c + 1)
                    pe.wait_ge(pt_sb, min(a - 1, NJ))
                    for t in range(4):
                        i = E.transpose(heads(2)[:, t, :], yn[:, t * P:(t + 1) * P], ident)
                    i.then_inc(yt_ps, 1)

            prep_decay(0)
            prep(0)
            pe.wait_ge(w_lo, U_IN + 10)
            mv_tile(0)
            prep_turn(0)
            mv_tile(1)
            att_stats(4)
            att_stats(5)
            prep_decay(1)
            prep(1)
            mv_tile(2)
            prep_turn(1)
            mv_tile(3)
            level_zero(0)
            for l in range(1, LEVELS):
                level_first(0, l)
                if l <= 4:
                    n = 10 + (l - 1) // 2
                    pe.wait_ge(w_lo, U_IN + n + 1)
                    in_tile(21 + l, n, (l - 1) % 2)
                if l == LAST - 1:
                    prep_decay(2)
                if l == LAST:
                    pe.wait_ge(p_evac, 26)
                    prep(2)
                level_second(0, l)
            for j in range(2):
                level_turn(0, LEVELS, j)
            prep_turn(2)
            prep_decay(3)
            pe.wait_ge(ratt_ready, 1)
            pe.wait_ge(xt_sb, n_t(1, 1, 0))
            for t in range(2):
                for c in range(NC_):
                    i = spread_pair(MK_BANKS[t], c * P, ratt[:, 2 + t, c, :], used=t == 0 and c == 0)
                i.then_inc(mkbc_ps, 1)
            pe.wait_ge(mk_ready, 2)
            pe.wait_ge(pt_ready, 3)
            pe.wait_ge(bv_ready, 12)
            pe.wait_ge(kt_ready, 12)
            pe.wait_ge(ck_ready, 1)
            attention(A_PREP)
            attention(A_PREP + 1)
            prep(3)
            attention(A_PREP + 2)
            prep_turn(3)
            for a in range(A_PREP + 3, A_LEVEL0):
                attention(a)
            level_zero(1)
            attention(A_LEVEL0)
            for l in range(1, LEVELS):
                level_first(1, l)
                attention(A_LEVEL + 2 * (l - 1))
                level_second(1, l)
                attention(A_LEVEL + 2 * (l - 1) + 1)
            for j in range(2):
                level_turn(1, LEVELS, j)
            attention(A_SCAN - 2)
            attention(A_SCAN - 1)
            pe.wait_ge(xt_sb, n_t(2, 1, 0))
            for a in range(A_SCAN, NJ + 4):
                if a >= A_SCAN + 4 * NC_:
                    attention(a)
                    continue
                c, s = (a - A_SCAN) // 4, (a - A_SCAN) % 4
                attention(a)
                cs = slice(c * P, (c + 1) * P)
                if s == 0 and c >= 1:
                    pe.wait_ge(s_upd, 4 * c)
                    for h in range(H):
                        i = E.matmul(heads(4)[:, h, :], qkv[:, 4 + h, cs], state[:, c % 2, h, :],
                                     start=True, stop=True)
                    i.then_inc(ks_ps, 1)
                if s == 1:
                    if c >= 1:
                        pe.wait_ge(r_sb, 4 * c)
                    for h in range(H):
                        rhs = rsb[:, h, :] if c >= 1 else qkv[:, 8 + h, cs]
                        i = E.matmul(heads(5)[:, h, :], xt[:, c, h, :], rhs, start=True, stop=True)
                    i.then_inc(v_ps, 1)
                if s == 2:
                    pe.wait_ge(v_sb, c + 1)
                    if c < NC_ - 1:
                        for h in range(H):
                            i = E.matmul(heads(7)[:, h, :], kt[:, c, h, :], vsb[:, h, :], start=True, stop=True)
                        i.then_inc(kv_ps, 1)
                    if c >= 1:
                        pe.wait_ge(o_sb, 2 * c)
                    for h in range(H):
                        if c >= 1:
                            E.matmul(heads(6)[:, h, :], state[:, c % 2, h, :], qkv[:, h, cs], start=True,
                                     stop=False)
                        i = E.matmul(heads(6)[:, h, :], vsb[:, h, :], pt[:, c, h, :], start=(c == 0), stop=True)
                    i.then_inc(o_ps, 1)
            pe.wait_ge(o_sb, 8)
            for h in range(H):
                for c in range(NC_):
                    m = h * NC_ + c
                    i = E.matmul(psum[0][:, m:m + 1], qkv[:, H + h, c * P:(c + 1) * P], ones[:, 0:1],
                                 start=True, stop=True)
            i.then_inc(o_stat, 1)

            order = [4, 5, 6, 7, 0, 1, 2, 3]

            def out_terms(d, ks, used=0):
                for k in ks:
                    terms = split_product(psum[4 + d % 4][:], wparts(U_OUT + d // 2, k, (d % 2) * P, P, 256),
                                          (ahi[:, k, :], alo[:, k, :]), order.index(k), KD - 1,
                                          used=used if k == order[0] else 0)
                return terms

            pe.wait_ge(w_lo, U_OUT + 2)
            pe.wait_ge(yb_lo, NC_)
            for d in range(2):
                out_terms(d, order[:4])
            pe.wait_ge(ro_ready, 1)
            for h in range(H):
                for c in range(NC_):
                    i = spread(h, c * P, gcol(G_B, h, c).broadcast_to([P, P]))
                i.then_inc(obc_ps, 1)
            for d in range(2, 4):
                out_terms(d, order[:4])
            for k in order[4:]:
                pe.wait_ge(y_lo, k + 1)
                for d in range(4):
                    i = out_terms(d, [k])
                    if k == order[-1]:
                        i.then_inc(wo_ps, 1)
            for d in range(4, KD):
                if d % 2 == 0:
                    pe.wait_ge(w_lo, U_OUT + d // 2 + 1)
                pe.wait_ge(xo_added, d - 3)
                out_terms(d, order, used={4: 2, 6: 1}.get(d, 0)).then_inc(wo_ps, 1)

            ffn(1, 2)


def constants():
    import numpy as np

    i = np.arange(P)
    c = np.zeros((P, C_N), np.float32)
    c[:, C_ID:C_ID + P] = np.eye(P)
    c[:, C_UP:C_UP + P] = i[:, None] <= i[None, :]
    c[:, C_ONE:C_ONE + P] = 1.0
    c[:, C_NEG:C_NEG + P] = np.where(i[:, None] <= i[None, :], 0.0, -1e30)
    for l in range(LEVELS):
        s = 1 << l
        same = (i[:, None] // (2 * s)) == (i[None, :] // (2 * s))
        c[:, C_LEV + l * P:C_LEV + (l + 1) * P] = same & (i[:, None] % (2 * s) < s) & (i[None, :] % (2 * s) >= s)
    rel = np.arange(T)[None, :] - (T - P) - i[:, None]
    c[:, C_REL:C_REL + T] = np.where(rel <= 0, rel, -1e30)
    c[:, C_SEL] = i < DH
    c[:, C_SEL + 1] = i >= DH
    return c


def columns(w, start, n):
    return w[:, start:start + n].reshape(KD, P, n).transpose(1, 0, 2).reshape(P, KD * n)


def kernel(**inputs):
    import numpy as np
    import concourse.bacc as bacc
    from concourse.bass_utils import run_bass_kernel_spmd

    a = {k: np.ascontiguousarray(v) for k, v in inputs.items()}

    def ffn_units(g, u, d):
        def down(i):
            return d[256 * i:256 * (i + 1)].reshape(2, P, D).transpose(1, 0, 2).reshape(P, 2 * D)

        units = [columns(g, 0, 256), columns(u, 0, 256)]
        for i in range(1, FG):
            units += [columns(g, 256 * i, 256), columns(u, 256 * i, 256), down(i - 1)]
        return units + [down(FG - 1)]

    w_in, w_out, w_kv = a["w_in"][0], a["w_out"][0], a["w_mem_kv"][0]
    starts = [256 * i for i in range(6)] + [2056, 2312, 2824, 2568] + [1536, 1792]
    units = [columns(w_kv, 0, 256), columns(w_kv, 256, 256)]
    units += ffn_units(a["ffn1_w_gate"][0], a["ffn1_w_up"][0], a["ffn1_w_down"][0])
    units += [columns(w_in, s, 256) for s in starts]
    units += [columns(w_out, 256 * i, 256) for i in range(4)]
    units += ffn_units(a["ffn2_w_gate"][0], a["ffn2_w_up"][0], a["ffn2_w_down"][0])

    def per_partition(v):
        return v.reshape(-1, P).T

    small = np.concatenate(
        [per_partition(a[n][0]) for n in ("ffn1_norm", "mix_norm", "ffn2_norm", "mem_norm")]
        + [a["gdn_conv_w"][0].reshape(4, 12, P).transpose(2, 1, 0).reshape(P, 48), a["gdn_out_norm"][0][:, None]]
        + [np.concatenate([a[n][0]] * 2)[:, None] for n in ("moba_q_norm", "moba_k_norm", "mem_q_norm", "mem_k_norm")]
        + [np.broadcast_to(a[n], (P, H)) for n in ("gdn_a_log", "gdn_dt_bias")], axis=1)
    arrays = {
        "stream": np.stack(units),
        "x_in": a["x"][0].T.reshape(KD, P, T).transpose(1, 0, 2),
        "mem_in": a["mem"][0].T.reshape(KD, P, M).transpose(1, 0, 2),
        "ab_in": w_in[:, 2048:2056].reshape(KD, P, 8).transpose(1, 0, 2),
        "small_in": small,
        "const_in": constants(),
    }
    arrays = {k: np.ascontiguousarray(v) for k, v in arrays.items()}
    nc = bacc.Bacc("TRN2", target_bir_lowering=False, num_devices=1)
    args = [nc.dram_tensor(k, v.shape, F32, kind="ExternalInput").ap() for k, v in arrays.items()]
    args.append(nc.dram_tensor("out", (P, KD, T), F32, kind="ExternalOutput").ap())
    build(nc, *args)
    got = run_bass_kernel_spmd(nc, [arrays], core_ids=[0]).results[0]["out"]
    return got.transpose(1, 0, 2).reshape(D, T).T.reshape(1, T, D)
```
